# Optimizing a Trainium2 kernel written in Bass

```python
import math
import jax, jax.numpy as jnp
from jax import lax
import numpy as np

D_MODEL = 1024
BATCH = 1
SEQ = 256
DEPTH = 1

RET_HEADS = 8
RET_HEAD_DIM = 128
RET_WIDTH = RET_HEADS * RET_HEAD_DIM
RET_CHUNK = 128
ROPE_BASE = 10000.0
GN_EPS = 1e-5
POOL_WINDOWS = (2, 4, 8, 16)
POOL_GROUPS = len(POOL_WINDOWS)
POOL_WIDTH = D_MODEL
POOL_GROUP = POOL_WIDTH // POOL_GROUPS
N_BRANCHES = 2
IN_WIDTH = 4 * RET_WIDTH + POOL_WIDTH + N_BRANCHES * D_MODEL
N_EXPERTS = 32
TOP_K = 4
D_FF = D_MODEL
SWIGLU_ALPHA = 1.702
SWIGLU_LIMIT = 7.0
EXPERT_BLOCK = 128
PLE_DIM = 256
RMS_EPS = 1e-6

kernel_name = "hybrid_retention_pool_moe_block"

def rms_norm(x, g):
    xf = x.astype(jnp.float32)
    y = xf * lax.rsqrt(jnp.mean(xf * xf, axis=-1, keepdims=True) + RMS_EPS)
    return (y * g.astype(jnp.float32)).astype(x.dtype)

def rotary(x, positions):
    half = x.shape[-1] // 2
    inv = ROPE_BASE ** (-jnp.arange(half, dtype=jnp.float32) / half)
    ang = positions.astype(jnp.float32)[..., None] * inv
    cos = jnp.cos(ang)[:, :, None, :]
    sin = jnp.sin(ang)[:, :, None, :]
    xf = x.astype(jnp.float32)
    x1, x2 = xf[..., :half], xf[..., half:]
    return jnp.concatenate([x1 * cos - x2 * sin, x2 * cos + x1 * sin], axis=-1)

def retention_chunkwise(q, k, v):
    B, S, H, Dh = q.shape
    N = S // RET_CHUNK
    log_gamma = jnp.log1p(-jnp.exp2(-5.0 - jnp.arange(H, dtype=jnp.float32)))
    qc = q.reshape(B, N, RET_CHUNK, H, Dh)
    kc = k.reshape(B, N, RET_CHUNK, H, Dh)
    vc = v.reshape(B, N, RET_CHUNK, H, Dh)
    idx = jnp.arange(RET_CHUNK, dtype=jnp.float32)
    diff = idx[:, None] - idx[None, :]
    causal = diff >= 0
    dmat = jnp.where(causal[None], jnp.exp(log_gamma[:, None, None] * jnp.where(causal, diff, 0.0)[None]), 0.0)
    scores = jnp.einsum('bnihd,bnjhd->bnhij', qc, kc) * dmat
    inner = jnp.einsum('bnhij,bnjhe->bnihe', scores, vc)
    zeta = jnp.exp(log_gamma[:, None] * (RET_CHUNK - 1.0 - idx)[None])
    kv = jnp.einsum('bnjhd,hj,bnjhe->nbhde', kc, zeta, vc)
    chunk_decay = jnp.exp(log_gamma * RET_CHUNK)[None, :, None, None]

    def step(state, kv_n):
        return state * chunk_decay + kv_n, state

    _, prev = lax.scan(step, jnp.zeros((B, H, Dh, Dh), q.dtype), kv)
    xi = jnp.exp(log_gamma[:, None] * (idx + 1.0)[None])
    cross = jnp.einsum('bnihd,nbhde,hi->bnihe', qc, prev, xi)
    return (inner + cross).reshape(B, S, H, Dh)

def pool_mixer(u, w_pool, pool_scale):
    B, S, C = u.shape
    uf = u.astype(jnp.float32)
    csum = jnp.cumsum(uf, axis=1)
    pos = jnp.arange(S)
    outs = []
    for gi, w in enumerate(POOL_WINDOWS):
        sl = slice(gi * POOL_GROUP, (gi + 1) * POOL_GROUP)
        c = csum[..., sl]
        lagged = jnp.pad(c, ((0, 0), (w, 0), (0, 0)))[:, :S]
        count = jnp.minimum(pos + 1, w).astype(jnp.float32)[None, :, None]
        mixed = ((c - lagged) / count - uf[..., sl]).astype(u.dtype)
        outs.append(jnp.einsum('bsc,cd->bsd', mixed, w_pool[gi]))
    return jnp.concatenate(outs, axis=-1) * pool_scale

def swiglu_clamped(gu):
    gate, up = gu[..., :D_FF], gu[..., D_FF:]
    gate = jnp.minimum(gate, SWIGLU_LIMIT)
    up = jnp.clip(up, -SWIGLU_LIMIT, SWIGLU_LIMIT)
    return (up + 1.0) * (gate * jax.nn.sigmoid(gate * SWIGLU_ALPHA))

def moe(h, w_router, b_router, w_gate_up, b_gate_up, w_down, b_down):
    B, S, D = h.shape
    T = B * S
    A = T * TOP_K
    xt = h.reshape(T, D)
    logits = (xt @ w_router + b_router).astype(jnp.float32)
    top_val, top_idx = lax.top_k(logits, TOP_K)
    top_w = jax.nn.softmax(top_val, axis=-1)
    flat_e = top_idx.reshape(A)
    flat_tok = (jnp.arange(A, dtype=jnp.int32) // TOP_K)
    flat_w = top_w.reshape(A)
    order = jnp.argsort(flat_e)
    sorted_e = flat_e[order]
    counts = jnp.bincount(flat_e, length=N_EXPERTS)
    padded = (counts + EXPERT_BLOCK - 1) // EXPERT_BLOCK * EXPERT_BLOCK
    starts = jnp.cumsum(counts) - counts
    pends = jnp.cumsum(padded)
    pstarts = pends - padded
    rank = jnp.arange(A, dtype=jnp.int32) - starts[sorted_e]
    dest = pstarts[sorted_e] + rank
    n_blocks = (A + EXPERT_BLOCK - 1) // EXPERT_BLOCK + N_EXPERTS
    P = n_blocks * EXPERT_BLOCK
    slot_tok = jnp.full((P,), T, jnp.int32).at[dest].set(flat_tok[order])
    slot_w = jnp.zeros((P,), jnp.float32).at[dest].set(flat_w[order])
    block_e = jnp.clip(jnp.searchsorted(pends, jnp.arange(n_blocks) * EXPERT_BLOCK, side='right'), 0, N_EXPERTS - 1)
    x_pad = jnp.concatenate([xt, jnp.zeros((1, D), xt.dtype)], axis=0)
    xb = x_pad[slot_tok].reshape(n_blocks, EXPERT_BLOCK, D)

    def expert_block(args):
        xblk, e = args
        act = swiglu_clamped(xblk @ w_gate_up[e] + b_gate_up[e])
        return act @ w_down[e] + b_down[e]

    yb = lax.map(expert_block, (xb, block_e)).reshape(P, D)
    yb = yb * slot_w[:, None].astype(yb.dtype)
    y = jnp.zeros((T + 1, D), yb.dtype).at[slot_tok].add(yb)[:T]
    return y.reshape(B, S, D)

def setup_inputs(seed: int = 0) -> dict:
    key = jax.random.key(seed)
    ks = jax.random.split(key, 24)
    f32 = jnp.float32
    nrm = lambda k, shape, scale: jax.random.normal(k, shape, f32) * scale
    L = DEPTH
    return {
        "x": nrm(ks[0], (BATCH, SEQ, D_MODEL), 1.0),
        "p": nrm(ks[1], (DEPTH, BATCH, SEQ, PLE_DIM), 1.0),
        "positions": jnp.broadcast_to(jnp.arange(SEQ, dtype=jnp.int32)[None], (BATCH, SEQ)),
        "g_mix_norm": 1.0 + nrm(ks[2], (L, D_MODEL), 0.05),
        "w_in": nrm(ks[3], (L, D_MODEL, IN_WIDTH), D_MODEL ** -0.5),
        "g_ret_norm": 1.0 + nrm(ks[4], (L, RET_WIDTH), 0.05),
        "w_pool": nrm(ks[5], (L, POOL_GROUPS, POOL_GROUP, POOL_GROUP), POOL_GROUP ** -0.5),
        "pool_scale": 1.0 + nrm(ks[6], (L, POOL_WIDTH), 0.05),
        "w_branch": nrm(ks[7], (L, N_BRANCHES, RET_WIDTH, D_MODEL), RET_WIDTH ** -0.5),
        "w_out": nrm(ks[8], (L, D_MODEL, D_MODEL), D_MODEL ** -0.5),
        "g_ffn_norm": 1.0 + nrm(ks[9], (L, D_MODEL), 0.05),
        "w_router": nrm(ks[10], (L, D_MODEL, N_EXPERTS), D_MODEL ** -0.5),
        "b_router": nrm(ks[11], (L, N_EXPERTS), 0.01),
        "w_gate_up": nrm(ks[12], (L, N_EXPERTS, D_MODEL, 2 * D_FF), D_MODEL ** -0.5),
        "b_gate_up": nrm(ks[13], (L, N_EXPERTS, 2 * D_FF), 0.01),
        "w_down": nrm(ks[14], (L, N_EXPERTS, D_FF, D_MODEL), D_FF ** -0.5),
        "b_down": nrm(ks[15], (L, N_EXPERTS, D_MODEL), 0.01),
        "g_ple_norm": 1.0 + nrm(ks[16], (L, D_MODEL), 0.05),
        "w_ple_gate": nrm(ks[17], (L, D_MODEL, D_MODEL), D_MODEL ** -0.5),
        "w_ple_proj": nrm(ks[18], (L, PLE_DIM, D_MODEL), PLE_DIM ** -0.5),
        "g_final": 1.0 + nrm(ks[19], (D_MODEL,), 0.05),
    }

def reference(x, p, positions, g_mix_norm, w_in, g_ret_norm, w_pool, pool_scale, w_branch, w_out,
              g_ffn_norm, w_router, b_router, w_gate_up, b_gate_up, w_down, b_down,
              g_ple_norm, w_ple_gate, w_ple_proj, g_final):
    B, S, D = x.shape
    for i in range(DEPTH):
        h = rms_norm(x, g_mix_norm[i])
        proj = h @ w_in[i]
        q, k, v, g_ret, u_pool, gate_a, gate_b = jnp.split(
            proj, np.cumsum([RET_WIDTH] * 4 + [POOL_WIDTH, D_MODEL]).tolist(), axis=-1)
        qh = rotary(q.reshape(B, S, RET_HEADS, RET_HEAD_DIM), positions)
        kh = rotary(k.reshape(B, S, RET_HEADS, RET_HEAD_DIM), positions) * (RET_HEAD_DIM ** -0.5)
        vh = v.reshape(B, S, RET_HEADS, RET_HEAD_DIM).astype(jnp.float32)
        ret = retention_chunkwise(qh, kh, vh)
        mu = jnp.mean(ret, axis=-1, keepdims=True)
        var = jnp.mean(jnp.square(ret - mu), axis=-1, keepdims=True)
        ret = ((ret - mu) * lax.rsqrt(var + GN_EPS)).reshape(B, S, RET_WIDTH)
        ret = (ret * g_ret_norm[i].astype(jnp.float32)).astype(x.dtype)
        y_ret = jax.nn.silu(g_ret) * ret
        y_pool = pool_mixer(u_pool, w_pool[i], pool_scale[i])
        branch_a = y_ret @ w_branch[i, 0]
        branch_b = y_pool @ w_branch[i, 1]
        merged = jax.nn.sigmoid(gate_a) * branch_a + jax.nn.sigmoid(gate_b) * branch_b
        x = x + merged @ w_out[i]
        h2 = rms_norm(x, g_ffn_norm[i])
        x = x + moe(h2, w_router[i], b_router[i], w_gate_up[i], b_gate_up[i], w_down[i], b_down[i])
        h3 = rms_norm(x, g_ple_norm[i])
        ple_gate = jax.nn.sigmoid(h3 @ w_ple_gate[i])
        x = x + ple_gate * (p[i].astype(x.dtype) @ w_ple_proj[i])
    return rms_norm(x, g_final)


_drawn_inputs = setup_inputs


def setup_inputs(seed=0):
    import zlib

    import numpy as np

    out = dict(_drawn_inputs(seed))
    spreads = {}
    factors = {'b_gate_up': 8.0, 'b_down': 8.0, 'g_ple_norm': 7.371}
    for name, (base, spread) in spreads.items():
        noise = np.random.default_rng([zlib.crc32(name.encode()), seed]).standard_normal(out[name].shape)
        drawn = base * np.exp(spread * noise) if base else spread * noise
        out[name] = __import__('jax').numpy.asarray(drawn.astype(out[name].dtype))
    for name, factor in factors.items():
        out[name] = (out[name] * factor).astype(out[name].dtype)
    return out
```

```python
from contextlib import ExitStack

import concourse.bass as bass
from concourse import mybir

F32 = mybir.dt.float32
I32 = mybir.dt.int32
ALU = mybir.AluOpType
ACT = mybir.ActivationFunctionType
AX = mybir.AxisListType

P = 128
SEQ, D = 256, 1024
TILES = SEQ // P
KD = D // P
HEADS = 8
N_EXPERTS, TOP_K = 32, 4
FF = 1024
PLE = 256
WINDOWS = (2, 4, 8, 16)
BLOCK = 64
BLOCKS_MAX = SEQ // BLOCK
RMS_EPS, GN_EPS = 1e-6, 1e-5
LIMIT, ALPHA = 7.0, 1.702
BIG = 3.0e38
TWO_PI_HI, TWO_PI_MID = 6.28125, 0.0019350051879882812
TWO_PI_LO = 6.283185307179586 - TWO_PI_HI - TWO_PI_MID
ROUND = 12582912.0

SLOTS, SLOT = 12, 2048
N = 512
Q, K_, V_, U, G_, GA, GB = range(7)
COLUMN_BLOCKS = [0, 1, 2, 3, 4, 5, 8, 9, 6, 7, 10, 11, 12, 13]
POOL_AFTER = 12


def block_chunk(j):
    return 2 * j + (j >= POOL_AFTER)


POOL_CHUNK = 2 * POOL_AFTER
BRANCH_CHUNK = 2 * len(COLUMN_BLOCKS) + 1
OUT_CHUNK = BRANCH_CHUNK + 8
EXPERT_CHUNK = OUT_CHUNK + 4
UP_CHUNKS, DOWN_CHUNKS = 8, 4
PER_EXPERT = UP_CHUNKS + DOWN_CHUNKS
PAIRS = N_EXPERTS // 2
PLE_CHUNK = EXPERT_CHUNK + N_EXPERTS * PER_EXPERT

IDENT, INVF = 0, P
EARLY = INVF + 64
TRI = EARLY
ONES = TRI + P
IOTA = ONES + P
DMAT = IOTA + BLOCKS_MAX * BLOCK + BLOCK
ZETA = DMAT + HEADS * P
XI = ZETA + HEADS
POOLM = XI + HEADS
N_CONST = POOLM + 3 * len(WINDOWS) * P

G_MIX, G_RET, G_POOL, G_FFN, G_PLE = (KD * i for i in range(5))


class ExpertSemaphores:

    def __init__(self, sem, tag, base, acc0):
        self.base, self.acc0 = base, acc0
        self.onehot_ready = sem(tag + "_onehot_ready")
        self.gathered = sem(tag + "_gathered")
        self.hg_ready = sem(tag + "_hg_ready")
        self.gate_ready = sem(tag + "_gate_ready")
        self.sig_ready = sem(tag + "_sig_ready")
        self.act_ready = sem(tag + "_act_ready")
        self.dT_ready = sem(tag + "_dT_ready")
        self.xposed = sem(tag + "_xposed")
        self.os_ready = sem(tag + "_os_ready")
        self.sw_ready = sem(tag + "_sw_ready")
        self.swt_done = sem(tag + "_swt_done")
        self.st_ready = sem(tag + "_st_ready")
        self.scattered = sem(tag + "_scattered")
        self.acc_done = sem(tag + "_acc_done")
        self.chunk_used = sem(tag + "_chunk_used")
        self.pair_done = sem(tag + "_pair_done")
        self.order = sem(tag + "_order")
        self.loaded = [sem(f"{tag}_loaded{i}") for i in range(SLOTS)]


class Count:

    def __init__(self):
        self.n, self.base = 0, 0

    def enter(self, turns_before, per_turn):
        self.start, self.per_turn, self.before = self.n, per_turn, self.n
        self.base, self.n = turns_before * per_turn, self.n

    def leave(self, turns):
        assert self.n - self.before == self.per_turn, (self.n - self.before, self.per_turn)
        self.base, self.n = 0, self.before + turns * self.per_turn

    def value(self):
        return self.base + self.n


def build(nc, t):
    ctx = ExitStack()
    with ctx:
        def sb(name, shape, dt=F32):
            return ctx.enter_context(nc.sbuf_tensor(name, shape, dt))

        def sem(name):
            return ctx.enter_context(nc.semaphore(name))

        ring = sb("ring", [P, SLOTS, SLOT])
        x = sb("x", [P, TILES, D])
        xn = sb("xn", [P, TILES, D])
        hT = sb("hT", [P, KD, SEQ])
        B = [sb(f"B{i}", [P, 2048]) for i in range(9)]
        const = sb("const", [P, N_CONST])
        vecs = sb("vecs", [P, 5 * KD])
        small = sb("small", [P, 64])
        ps = ctx.enter_context(nc.psum_tensor("ps", [P, 8, N], F32))

        ident = const[:, IDENT:IDENT + P]
        tri = const[:, TRI:TRI + P]
        ones = const[:, ONES:ONES + P]

        def rows(buf, width=D):
            return buf[:, 0:TILES * width].rearrange("p (t n) -> p t n", t=TILES)

        def cols(buf):
            return buf[:, :].rearrange("p (k s) -> p k s", k=KD)

        q, ret = rows(B[0]), rows(B[0])
        k = rows(B[1])
        scoresT = B[1][:, D:2 * D].rearrange("p (c n) -> p c n", c=TILES)
        square, merged = rows(B[1]), rows(B[1])
        v, mixedT = rows(B[2]), cols(B[2])
        qT, yretT = cols(B[3]), cols(B[3])
        kT, ypoolT = cols(B[4]), cols(B[4])
        rot_a, rot_b = B[4][:, 0:N], B[4][:, N:2 * N]
        silu_g, mergedT = rows(B[5]), cols(B[5])
        kv, cross = B[6][:, 0:N], B[6][:, N:2 * N]
        gates = [rows(B[6]), rows(B[7])]
        u = rows(B[8])
        branch_tmp = B[0][:, 0:N]
        vec_rows = B[6][0:5 * KD, 0:P]
        pos_int = B[6][0:TILES, P:2 * P].bitcast(I32)
        pos_row = B[6][0:TILES, 2 * P:3 * P]
        angle = B[7][:, 0:P].rearrange("p (t f) -> p t f", t=TILES)
        turns = B[7][:, P:2 * P].rearrange("p (t f) -> p t f", t=TILES)
        cos = B[8][:, 2 * P:3 * P].rearrange("p (t f) -> p t f", t=TILES)
        sin = B[8][:, 3 * P:4 * P].rearrange("p (t f) -> p t f", t=TILES)
        nsin = B[8][:, 4 * P:5 * P].rearrange("p (t f) -> p t f", t=TILES)
        waste = B[8][:, D:2 * D]
        hg = [B[0][:, i * N:(i + 1) * N].rearrange("p (k s) -> p k s", k=KD) for i in range(2)]
        act = B[0][:, 2 * N:3 * N].rearrange("p (k s) -> p k s", k=KD)
        gate, up, sig, prod = (z.rearrange("p (k s) -> p k s", k=KD) for z in
                               (B[0][:, 3 * N:4 * N], B[1][:, 0:N], B[1][:, N:2 * N], B[1][:, 2 * N:3 * N]))
        p_in = B[1][:, 3 * N:4 * N].rearrange("p (t n) -> p t n", t=TILES)
        bgu_rows = B[2][0:N_EXPERTS, :]
        dT = B[2][:, 0:D]
        slot_rows = B[2][:, D:2 * D]
        scatterT = B[3][:, 0:SEQ]
        onehot = [B[3][:, 256 + i * P:256 + (i + 1) * P].rearrange("p (t s) -> p t s", t=TILES) for i in range(2)]
        weighted = B[3][:, 512:768].rearrange("p (t s) -> p t s", t=TILES)
        pT = B[3][:, 1024:1536].rearrange("p (c s) -> p c s", c=2)
        bgu = B[3][:, 1536:2048].rearrange("p (e m) -> p e m", m=16)
        EP = N_EXPERTS + 2
        at = [0]

        def piece(n):
            at[0] += n
            return B[4][:, at[0] - n:at[0]]

        combT = piece(SEQ)[0:N_EXPERTS, :]
        rank = piece(TILES * EP).rearrange("p (t e) -> p t e", t=TILES)
        comb = piece(TILES * EP).rearrange("p (t e) -> p t e", t=TILES)
        logit = piece(TILES * 36).rearrange("p (t e) -> p t e", t=TILES)
        marked = piece(TILES * 36).rearrange("p (t e) -> p t e", t=TILES)
        top = piece(TILES * 8).rearrange("p (t e) -> p t e", t=TILES)
        mask = piece(TILES * N_EXPERTS).rearrange("p (t e) -> p t e", t=TILES)
        expo = piece(TILES * N_EXPERTS).rearrange("p (t e) -> p t e", t=TILES)
        counts = piece(N_EXPERTS)[0:1, :].bitcast(I32)
        count_f = piece(N_EXPERTS)[0:1, :]
        count_top = piece(1)[0:1, :].bitcast(I32)
        count_top_f = piece(1)[0:1, :]
        w_router = piece(KD * N_EXPERTS).rearrange("p (k e) -> p k e", k=KD)
        b_router = piece(N_EXPERTS)[0:1, :]
        assert at[0] <= 2048
        w_proj = B[6][:, :].rearrange("p (c n) -> p c n", c=2)
        ple = rows(B[7])
        b_down = B[8][0:N_EXPERTS, 0:D]
        g_final = B[8][:, D:2 * D]
        result = rows(B[0])
        ple_gate = B[1][:, 0:2 * N].rearrange("p (t n) -> p t n", t=TILES)

        pos, ss, rstd, neg, tot = (small[:, 2 * i:2 * i + 2] for i in range(5))
        mean, var, exponent = (small[:, i:i + 16] for i in (16, 32, 48))

        x_loaded, vec_loaded, early_loaded, const_loaded = map(sem, ("x_loaded", "vec_loaded", "early_loaded", "const_loaded"))
        router_loaded, late_loaded, bgu_loaded = map(sem, ("router_loaded", "late_loaded", "bgu_loaded"))
        p_loaded, proj_loaded, stored = map(sem, ("p_loaded", "proj_loaded", "stored"))
        vec_order = sem("vec_order")
        pos_cast, vec_psum, vecs_read = map(sem, ("pos_cast", "vec_psum", "vecs_read"))
        angles_ready, sin_ready = sem("angles_ready"), sem("sin_ready")
        ss_ready, xn_ready, xT_psum, hT_ready = map(sem, ("ss_ready", "xn_ready", "xT_psum", "hT_ready"))
        var_ready, mean_square, rstd_ready = sem("var_ready"), sem("mean_square"), sem("rstd_ready")
        read_dve, read_act = sem("read_dve"), sem("read_act")
        rotated, qkT_psum, qkT_ready, kz_ready = map(sem, ("rotated", "qkT_psum", "qkT_ready", "kz_ready"))
        ret_psum, scores_ready, kv_ready, ret_read = map(sem, ("ret_psum", "scores_ready", "kv_ready", "ret_read"))
        square_in, squared, sig_g = sem("square_in"), sem("squared"), sem("sig_g")
        pool_psum, mixT_ready, ypT_ready = map(sem, ("pool_psum", "mixT_ready", "ypT_ready"))
        yret_ready, yrT_psum, yrT_ready = map(sem, ("yret_ready", "yrT_psum", "yrT_ready"))
        branch_read, mT_psum, mT_ready, x_ready = map(sem, ("branch_read", "mT_psum", "mT_ready", "x_ready"))
        logits_psum, exp_in, exp_ready = map(sem, ("logits_psum", "exp_in", "exp_ready"))
        mask_ready, comb_ready, route_psum, route_ready = map(sem, ("mask_ready", "comb_ready", "route_psum", "route_ready"))
        bias_psum, bias_read = sem("bias_psum"), sem("bias_read")
        pT_psum, pT_ready, ple_psum = sem("pT_psum"), sem("pT_ready"), sem("ple_psum")
        gate_sig, out_ready = sem("gate_sig"), sem("out_ready")

        first = ExpertSemaphores(sem, "first", EXPERT_CHUNK, 4)
        more = ExpertSemaphores(sem, "more", 0, 0)
        used, loaded = first.chunk_used, first.loaded

        block = ctx.enter_context(nc.Block())

        def two_banks(b):
            return ps[:, b:b + 2, :].rearrange("p b n -> p (b n)")

        def bank_cols(b, n=KD):
            return ps[:, b, :].rearrange("p (k s) -> p k s", k=n)

        def across(ap, n):
            return ap.unsqueeze(2).to_broadcast([P, ap.shape[1], n])

        def block_read(j):
            dve_blocks = [0, 1, 2, 3, 8, 9]
            if j in dve_blocks:
                return read_dve, 2 * (dve_blocks.index(j) + 1)
            act_blocks = [4, 5, 6, 7, 10, 11, 12, 13]
            return read_act, 2 * (act_blocks.index(j) + 1)

        def slot_of(c):
            return c % SLOTS

        def chunk_ready(eng, c):
            eng.wait_ge(loaded[slot_of(c)], 16 * (c // SLOTS + 1))

        def expert_ready(eng, s, pair, h, i):
            c = s.base + h * PER_EXPERT + i
            eng.wait_ge(s.loaded[slot_of(c)], 16 * (c // SLOTS + 1) + 32 * pair)

        left_body = {n: sem(f"left_body_{n}") for n in ("sp", "pe", "act", "dve")}

        def more_pairs(name, eng, body, skipped):
            top_count = eng.value_load(count_top[0:1, 0:1], min_val=0, max_val=SEQ)
            with eng.If(top_count > BLOCK):
                with eng.Fori(0, N_EXPERTS) as e:
                    for half in range(2):
                        low = (1 + 2 * half) * BLOCK
                        n_tokens = eng.value_load(counts[0:1, bass.ds(e, 1)], min_val=0, max_val=SEQ)
                        with eng.If(n_tokens > low):
                            body(2 * e + half, e, low)
                            eng.sem_inc(left_body[name], 1)
                        with eng.Else():
                            skipped()
                        eng.nop()
                eng.nop()
            eng.nop()

        @block.sync
        def _(sp):
            def load(c, src, shape=None):
                if c >= SLOTS:
                    sp.wait_ge(used, c - SLOTS + 1)
                dst = ring[:, slot_of(c), :]
                if shape:
                    dst = dst.rearrange("p (k n) -> p k n", k=shape)
                sp.dma_start(dst, src).then_inc(loaded[slot_of(c)], 16)

            w_in = t["w_in"][0].rearrange("(k p) n -> p k n", p=P)
            for j, cb in enumerate(COLUMN_BLOCKS):
                if j == POOL_AFTER:
                    load(POOL_CHUNK, t["w_pool"][0].rearrange("g (k p) n -> p (g k) n", p=P), 8)
                for half in range(2):
                    load(block_chunk(j) + half, w_in[:, 4 * half:4 * half + 4, cb * N:(cb + 1) * N], 4)
            for unit in range(4):
                w = t["w_branch"][0, 1 - unit % 2].rearrange("(k p) n -> p k n", p=P)
                for half in range(2):
                    load(BRANCH_CHUNK + 2 * unit + half,
                         w[:, 4 * half:4 * half + 4, (unit // 2) * N:(unit // 2 + 1) * N], 4)
            w_out = t["w_out"][0].rearrange("(k p) n -> p k n", p=P)
            for n in range(2):
                for half in range(2):
                    load(OUT_CHUNK + 2 * n + half, w_out[:, 4 * half:4 * half + 4, n * N:(n + 1) * N], 4)

            def load_expert(s, pair, h, e, first_turn=False):
                for i in range(PER_EXPERT):
                    c = s.base + h * PER_EXPERT + i
                    if c >= SLOTS:
                        sp.wait_ge(s.chunk_used, 24 * pair + c - SLOTS + 1)
                    elif not first_turn:
                        pass
                    dst = ring[:, slot_of(c), :]
                    if i < UP_CHUNKS:
                        src = t["w_gate_up"][0, bass.ds(e, 1), i * P:(i + 1) * P, :].rearrange("e p n -> p (e n)")
                    else:
                        r = (i - UP_CHUNKS) * 2 * P
                        src = t["w_down"][0, bass.ds(e, 1), r:r + 2 * P, :].rearrange("e (k p) n -> p (e k) n", p=P)
                        dst = dst.rearrange("p (k n) -> p k n", k=2)
                    sp.dma_start(dst, src).then_inc(s.loaded[slot_of(c)], 16)

            with sp.Fori(0, PAIRS) as pair:
                for h in range(2):
                    load_expert(first, pair, h, 2 * pair + h)

            def body(j, e, low):
                load_expert(more, j, 0, e)
                load_expert(more, j, 1, e)
                sp.wait_ge(more.pair_done, j + 1)

            def skipped():
                for s in range(SLOTS):
                    sp.sem_inc(more.loaded[s], 32)

            sp.wait_ge(route_ready, 1)
            sp.wait_ge(used, PLE_CHUNK)
            more_pairs("sp", sp, body, skipped)
            w_gate = t["w_ple_gate"][0].rearrange("(k p) n -> p k n", p=P)
            for n in range(2):
                for half in range(2):
                    load(PLE_CHUNK + 2 * n + half, w_gate[:, 4 * half:4 * half + 4, n * N:(n + 1) * N], 4)
            for i in range(TILES):
                sp.wait_ge(out_ready, i + 1)
                sp.dma_start(t["y"][0, i * P:(i + 1) * P, :], result[:, i, :]).then_inc(stored, 16)
            sp.wait_ge(stored, 16 * TILES)

        @block.tensor
        def _(pe):
            def mm(out, lhsT, rhs, start, stop):
                return pe.matmul(out, lhsT, rhs, start=start, stop=stop, skip_group_check=True)

            def transpose16(src, done, free=None):
                for j in range(KD // 2):
                    if free:
                        pe.wait_ge(free[0], free[1] + j)
                    for kk in range(2):
                        for i in range(TILES):
                            c = 2 * j + kk
                            last = pe.transpose(ps[:, 4 + j, kk * SEQ + i * P:kk * SEQ + (i + 1) * P],
                                                src[:, i, c * P:(c + 1) * P], ident)
                    last.then_inc(done, 1)

            def project(c0, lhsT, n_bank, first_ready=None, then_ready=None):
                for half in range(2):
                    wait = then_ready if half else first_ready
                    if wait:
                        pe.wait_ge(*wait)
                    chunk_ready(pe, c0 + half)
                    w = ring[:, slot_of(c0 + half), :].rearrange("p (k n) -> p k n", k=4)
                    for i in range(TILES):
                        for kk in range(4):
                            c = 4 * half + kk
                            last = mm(ps[:, n_bank + i, :], lhsT[:, c, i * P:(i + 1) * P], w[:, kk, :],
                                      c == 0, c == KD - 1)
                    last.then_inc(used, 1)

            pe.wait_ge(early_loaded, 16)
            pe.wait_ge(vec_loaded, 16 * 6)
            pe.transpose(ps[:, 0, 0:5 * KD], vec_rows, ident[0:5 * KD, 0:5 * KD])
            pe.wait_ge(pos_cast, 1)
            pe.transpose(ps[:, 0, 64:64 + TILES], pos_row, ident[0:TILES, 0:TILES]).then_inc(vec_psum, 1)

            pe.wait_ge(xn_ready, TILES)
            transpose16(xn, xT_psum)

            def column_block(j):
                if j == 0:
                    pe.wait_ge(vecs_read, 1)
                    pe.wait_ge(hT_ready, 4)
                if j >= 2:
                    pe.wait_ge(*block_read(j - 2))
                project(block_chunk(j), hT, 2 * (j % 2))

            def scores(g):
                if g == 0:
                    pe.wait_ge(qkT_ready, 8)
                    pe.wait_ge(kz_ready, 1)
                    pe.wait_ge(read_act, 2 * 2)
                else:
                    pe.wait_ge(ret_read, g)
                for c in range(TILES):
                    for i in range(4):
                        h = 4 * g + i
                        last = mm(ps[:, 4 + c, i * P:(i + 1) * P], kT[:, h, c * P:(c + 1) * P],
                                  qT[:, h, c * P:(c + 1) * P], True, True)
                    last.then_inc(ret_psum, 1)
                if g:
                    pe.wait_ge(kv_ready, g)
                for i in range(4):
                    h = 4 * g + i
                    last = mm(ps[:, 6, i * P:(i + 1) * P], k[:, 0, h * P:(h + 1) * P],
                              v[:, 0, h * P:(h + 1) * P], True, True)
                last.then_inc(ret_psum, 1)

            def inner(g):
                pe.wait_ge(scores_ready, 2 * g + 2)
                for c in range(TILES):
                    for i in range(4):
                        h = 4 * g + i
                        last = mm(ps[:, 4 + c, i * P:(i + 1) * P], scoresT[:, c, i * P:(i + 1) * P],
                                  v[:, c, h * P:(h + 1) * P], True, True)
                last.then_inc(ret_psum, 1)
                pe.wait_ge(kv_ready, g + 1)
                for i in range(4):
                    h = 4 * g + i
                    last = mm(ps[:, 7, i * P:(i + 1) * P], qT[:, h, P:2 * P], kv[:, i * P:(i + 1) * P], True, True)
                last.then_inc(ret_psum, 1)

            def pool_mix():
                pe.wait_ge(ret_read, 2)
                for j in range(4):
                    for kk in range(2):
                        c = 2 * j + kk
                        m = POOLM + 3 * P * (c // 2)
                        out = ps[:, 4 + j, kk * SEQ:(kk + 1) * SEQ]
                        uc = [u[:, i, c * P:(c + 1) * P] for i in range(TILES)]
                        mm(out[:, 0:P], uc[0], const[:, m:m + P], True, True)
                        mm(out[:, P:2 * P], uc[0], const[:, m + P:m + 2 * P], True, False)
                        last = mm(out[:, P:2 * P], uc[1], const[:, m + 2 * P:m + 3 * P], False, True)
                    last.then_inc(pool_psum, 1)

            def pool_project():
                pe.wait_ge(mixT_ready, 4)
                chunk_ready(pe, POOL_CHUNK)
                w = ring[:, slot_of(POOL_CHUNK), :].rearrange("p (k n) -> p k n", k=8)
                for m in range(KD):
                    for kk in range(2):
                        last = mm(ps[:, 4 + m // 2, (m % 2) * SEQ:(m % 2 + 1) * SEQ],
                                  w[:, 2 * (m // 2) + kk, (m % 2) * P:(m % 2 + 1) * P],
                                  mixedT[:, 2 * (m // 2) + kk, :], kk == 0, kk == 1)
                last.then_inc(used, 1)

            for j in range(4):
                column_block(j)
            pe.wait_ge(const_loaded, 16)
            column_block(4)
            pe.wait_ge(rotated, 4)
            transpose16(q, qkT_psum)
            column_block(5)
            pe.wait_ge(rotated, 8)
            transpose16(k, qkT_psum, free=(qkT_ready, 1))
            column_block(6)
            scores(0)
            column_block(7)
            inner(0)
            column_block(8)
            scores(1)
            column_block(9)
            inner(1)
            column_block(10)
            pool_mix()
            column_block(11)
            pool_project()
            column_block(12)
            column_block(13)
            pe.wait_ge(yret_ready, 1)
            transpose16(ret, yrT_psum, free=(ypT_ready, 1))

            for unit in range(4):
                if unit < 2:
                    pe.wait_ge(*block_read(12 + unit))
                else:
                    pe.wait_ge(branch_read, unit - 1)
                pe.wait_ge(yrT_ready, 4) if unit == 1 else None
                project(BRANCH_CHUNK + 2 * unit, yretT if unit % 2 else ypoolT, 2 * (unit % 2))
                if unit == 2 or unit == 3:
                    pe.wait_ge(branch_read, 2 * unit - 2)
                    for j in (2 * unit - 4, 2 * unit - 3):
                        for kk in range(2):
                            for i in range(TILES):
                                c = 2 * j + kk
                                last = pe.transpose(ps[:, 4 + j, kk * SEQ + i * P:kk * SEQ + (i + 1) * P],
                                                    merged[:, i, c * P:(c + 1) * P], ident)
                        last.then_inc(mT_psum, 1)
            project(OUT_CHUNK, mergedT, 0, (mT_ready, 2), (mT_ready, 4))
            project(OUT_CHUNK + 2, mergedT, 2)

            pe.wait_ge(bgu_loaded, 16)
            pe.wait_ge(x_ready, TILES)
            for m in range(2 * KD):
                last = pe.transpose(ps[:, 3, m * N_EXPERTS:(m + 1) * N_EXPERTS],
                                    bgu_rows[:, m * P:(m + 1) * P], ident[0:N_EXPERTS, 0:N_EXPERTS])
            last.then_inc(route_psum, 1)
            pe.wait_ge(xn_ready, 2 * TILES)
            transpose16(xn, xT_psum)
            pe.wait_ge(hT_ready, 8)
            pe.wait_ge(router_loaded, 32)
            for i in range(TILES):
                out = ps[:, 0, i * N_EXPERTS:(i + 1) * N_EXPERTS]
                for c in range(KD):
                    mm(out, hT[:, c, i * P:(i + 1) * P], w_router[:, c, :], c == 0, False)
                last = mm(out, ones[0:1, :], b_router, False, True)
            last.then_inc(logits_psum, 1)
            pe.wait_ge(mask_ready, 1)
            out = ps[:, 1, 0:N_EXPERTS]
            mm(out, tri, mask[:, 0, :], True, True)
            out = ps[:, 1, N_EXPERTS:2 * N_EXPERTS]
            mm(out, ones, mask[:, 0, :], True, False)
            mm(out, tri, mask[:, 1, :], False, True)
            out = ps[0:1, 1, 2 * N_EXPERTS:3 * N_EXPERTS]
            mm(out, ones[:, 0:1], mask[:, 0, :], True, False)
            mm(out, ones[:, 0:1], mask[:, 1, :], False, True).then_inc(route_psum, 1)
            pe.wait_ge(comb_ready, 1)
            for i in range(TILES):
                last = pe.transpose(ps[0:N_EXPERTS, 2, i * P:(i + 1) * P], comb[:, i, 0:N_EXPERTS], ident)
            last.then_inc(route_psum, 1)

            def gather(s, qi, par):
                pe.wait_ge(s.onehot_ready, qi + 1)
                for c in range(KD):
                    for i in range(TILES):
                        last = mm(ps[:, 4, c * BLOCK:(c + 1) * BLOCK], xn[:, i, c * P:(c + 1) * P],
                                  onehot[par][:, i, :], i == 0, i == TILES - 1)
                last.then_inc(s.gathered, 1)

            def gate_up(s, pair, h):
                pe.wait_ge(s.hg_ready, 2 * pair + h + 1)
                for c in range(UP_CHUNKS):
                    expert_ready(pe, s, pair, h, c)
                    w = ring[:, slot_of(s.base + h * PER_EXPERT + c), :]
                    for m in range(2 * KD):
                        last = mm(ps[:, m // KD, (m % KD) * BLOCK:(m % KD + 1) * BLOCK], w[:, m * P:(m + 1) * P],
                                  hg[h][:, c, :], c == 0 and m % KD == 0, c == UP_CHUNKS - 1)
                    last.then_inc(s.chunk_used, 1)

            def down(s, pair, h):
                pe.wait_ge(s.act_ready, 2 * pair + h + 1)
                for i in range(DOWN_CHUNKS):
                    expert_ready(pe, s, pair, h, UP_CHUNKS + i)
                    w = ring[:, slot_of(s.base + h * PER_EXPERT + UP_CHUNKS + i), :]
                    for kk in range(2):
                        c = 2 * i + kk
                        for n in range(KD):
                            last = mm(ps[:, 2 + n // 4, (n % 4) * P + h * BLOCK:(n % 4) * P + (h + 1) * BLOCK],
                                      w[:, kk * D + n * P:kk * D + (n + 1) * P], act[:, c, :],
                                      c == 0 and n % 4 == 0, c == KD - 1)
                    last.then_inc(s.chunk_used, 1)

            def scatter_weights(s, pair):
                pe.wait_ge(s.sw_ready, pair + 1)
                for i in range(TILES):
                    last = pe.transpose(ps[:, 7, i * P:(i + 1) * P], weighted[:, i, :], ident)
                last.then_inc(s.swt_done, 1)

            def to_rows(s, pair):
                pe.wait_ge(s.dT_ready, pair + 1)
                for n in range(KD):
                    last = pe.transpose(ps[:, 5 + n // 4, (n % 4) * P:(n % 4 + 1) * P], dT[:, n * P:(n + 1) * P], ident)
                last.then_inc(s.xposed, 1)

            def scatter(s, pair):
                pe.wait_ge(s.st_ready, pair + 1)
                pe.wait_ge(s.os_ready, pair + 1)
                for i in range(4):
                    if i == 3:
                        pe.wait_ge(s.acc_done, s.acc0 + 4 * pair + 1)
                    tile, n = i // 2, i % 2
                    mm(ps[:, (7, 5, 6, 7)[i], :], scatterT[:, tile * P:(tile + 1) * P],
                       slot_rows[:, n * N:(n + 1) * N], True, True).then_inc(s.scattered, 1)

            def pair_steps(pair, is_first=False):
                gate_up(first, pair, 0)
                gather(first, 2 * pair + 1, 1)
                if is_first:
                    pe.wait_ge(p_loaded, 16)
                    pe.wait_ge(proj_loaded, 16)
                    for c in range(2):
                        for i in range(TILES):
                            last = pe.transpose(ps[:, 5, c * SEQ + i * P:c * SEQ + (i + 1) * P],
                                                p_in[:, i, c * P:(c + 1) * P], ident)
                    last.then_inc(pT_psum, 1)
                    pe.wait_ge(pT_ready, 1)
                    for i in range(4):
                        tile, n = i // 2, i % 2
                        if i == 3:
                            pe.wait_ge(first.acc_done, 1)
                        for c in range(2):
                            last = mm(ps[:, (7, 5, 6, 7)[i], :], pT[:, c, tile * P:(tile + 1) * P],
                                      w_proj[:, c, n * N:(n + 1) * N], c == 0, c == 1)
                        last.then_inc(ple_psum, 1)
                else:
                    pe.wait_ge(first.acc_done, 4 * pair)
                    to_rows(first, pair - 1)
                    scatter(first, pair - 1)
                down(first, pair, 0)
                gate_up(first, pair, 1)
                gather(first, 2 * pair + 2, 0)
                pe.wait_ge(first.acc_done, 4 * pair + 4)
                scatter_weights(first, pair)
                down(first, pair, 1)

            pe.wait_ge(route_ready, 1)
            gather(first, 0, 0)
            for i in range(4):
                tile, n = i // 2, i % 2
                mm(ps[:, (0, 1, 5, 6)[i], :], combT[:, tile * P:(tile + 1) * P], b_down[:, n * N:(n + 1) * N],
                   True, True).then_inc(bias_psum, 1)
            pe.wait_ge(bias_read, 4)
            pair_steps(0, True)
            with pe.Fori(1, PAIRS) as pair:
                pair_steps(pair)
            pe.wait_ge(first.acc_done, 4 * PAIRS)
            to_rows(first, PAIRS - 1)
            scatter(first, PAIRS - 1)

            def body(j, e, low):
                pe.wait_ge(first.acc_done, first.acc0 + 4 * PAIRS)
                gather(more, 2 * j, 0)
                gate_up(more, j, 0)
                gather(more, 2 * j + 1, 1)
                down(more, j, 0)
                gate_up(more, j, 1)
                scatter_weights(more, j)
                down(more, j, 1)
                to_rows(more, j)
                scatter(more, j)
                pe.wait_ge(more.pair_done, j + 1)

            def skipped():
                for s, n in ((more.gathered, 2), (more.chunk_used, 24), (more.swt_done, 1),
                             (more.xposed, 1), (more.scattered, 4)):
                    pe.sem_inc(s, n)

            more_pairs("pe", pe, body, skipped)

            pe.wait_ge(xn_ready, 3 * TILES)
            transpose16(xn, xT_psum)
            pe.wait_ge(hT_ready, 12)
            project(PLE_CHUNK, hT, 0)
            project(PLE_CHUNK + 2, hT, 2)

        @block.gpsimd
        def _(pool):
            nc.gpsimd.memset(exponent, -0.5).then_inc(mean_square, 1)
            for turn in range(5):
                if turn == 1:
                    pool.wait_ge(var_ready, 1)
                    src, dst, n, eps = var, var, P, GN_EPS
                else:
                    pool.wait_ge(ss_ready, TILES * (turn + (turn == 0)))
                    src, dst, n, eps = ss, rstd, D, RMS_EPS
                nc.gpsimd.tensor_scalar(dst, src, 1.0 / n, eps, ALU.mult, ALU.add).then_inc(mean_square, 1)
                pool.wait_ge(mean_square, turn + 2)
                nc.gpsimd.tensor_tensor(dst, dst, exponent[:, 0:dst.shape[1]], ALU.pow).then_inc(rstd_ready, 1)

        @block.scalar
        def _(act_eng):
            e = act_eng
            e.dma_start(const[:, 0:EARLY], t["const"][:, 0:EARLY]).then_inc(early_loaded, 16)
            e.dma_start(x[:, :, :], t["x"][0].rearrange("(i p) n -> p i n", p=P)).then_inc(x_loaded, 16)
            for i, g in enumerate((t["g_mix_norm"], t["g_ret_norm"], t["pool_scale"], t["g_ffn_norm"], t["g_ple_norm"])):
                e.dma_start(vec_rows[KD * i:KD * (i + 1), :], g[0].rearrange("(k p) -> k p", p=P)).then_inc(vec_loaded, 16)
            e.dma_start(pos_int, t["positions"][0].rearrange("(i p) -> i p", p=P)).then_inc(vec_loaded, 16)
            e.dma_start(const[:, EARLY:], t["const"][:, EARLY:]).then_inc(const_loaded, 16)

            e.wait_ge(x_loaded, 16)
            for i in range(TILES):
                if i:
                    e.wait_ge(ss_ready, i)
                nc.scalar.activation(waste, x[:, i, :], ACT.Square, accum_out=ss[:, i:i + 1]).then_inc(ss_ready, 1)
            e.wait_ge(angles_ready, 1)
            nc.scalar.activation(sin, angle, ACT.Sin).then_inc(sin_ready, 1)
            nc.scalar.activation(cos, turns, ACT.Sin).then_inc(sin_ready, 1)

            def copies_qk(n):
                for j in range(4):
                    e.wait_ge(qkT_psum, 4 * n + j + 1)
                    nc.scalar.copy((qT, kT)[n][:, 2 * j:2 * j + 2, :], bank_cols(4 + j, 2)).then_inc(qkT_ready, 1)

            def read_block(j, dst, func):
                n = j % 2
                e.wait_ge(used, block_chunk(j) + 2)
                for i in range(TILES):
                    nc.scalar.activation(dst[:, i, n * N:(n + 1) * N], ps[:, 2 * n + i, :], func).then_inc(read_act, 1)

            def read_kv(g):
                e.wait_ge(ret_psum, 5 * g + 3)
                nc.scalar.copy(kv, ps[:, 6, :]).then_inc(kv_ready, 1)

            read_block(4, v, ACT.Copy)
            copies_qk(0)
            read_block(5, v, ACT.Copy)
            copies_qk(1)
            e.wait_ge(rotated, 8)
            read_block(6, u, ACT.Copy)
            read_kv(0)
            read_block(7, u, ACT.Copy)

            def silu_block(j):
                n = j % 2
                e.wait_ge(used, block_chunk(j) + 2)
                for i in range(TILES):
                    nc.scalar.activation(silu_g[:, i, n * N:(n + 1) * N], ps[:, 2 * n + i, :], ACT.Sigmoid).then_inc(sig_g, 1)

            silu_block(8)
            e.wait_ge(ret_read, 1)
            read_kv(1)
            silu_block(9)
            e.wait_ge(ret_read, 2)
            read_block(10, gates[0], ACT.Sigmoid)
            for j in range(4):
                e.wait_ge(pool_psum, j + 1)
                nc.scalar.copy(mixedT[:, 2 * j:2 * j + 2, :], bank_cols(4 + j, 2)).then_inc(mixT_ready, 1)
            e.dma_start(b_down, t["b_down"][0]).then_inc(late_loaded, 16)
            e.dma_start(g_final, t["g_final"].unsqueeze(0).to_broadcast([P, D])).then_inc(late_loaded, 16)
            e.wait_ge(square_in, 1)
            nc.scalar.activation(square, ret, ACT.Square).then_inc(squared, 1)
            read_block(11, gates[0], ACT.Sigmoid)
            e.wait_ge(used, POOL_CHUNK + 1)
            e.dma_start(bgu_rows, t["b_gate_up"][0]).then_inc(bgu_loaded, 16)
            read_block(12, gates[1], ACT.Sigmoid)
            read_block(13, gates[1], ACT.Sigmoid)
            for j in range(4):
                e.wait_ge(mT_psum, j + 1)
                nc.scalar.copy(mergedT[:, 2 * j:2 * j + 2, :], bank_cols(4 + j, 2)).then_inc(mT_ready, 1)
            e.wait_ge(branch_read, 4)
            e.dma_start(w_router, t["w_router"][0].rearrange("(k p) n -> p k n", p=P)).then_inc(router_loaded, 16)
            e.dma_start(b_router, t["b_router"]).then_inc(router_loaded, 16)
            e.dma_start(w_proj, t["w_ple_proj"][0].rearrange("(c p) n -> p c n", p=P)).then_inc(proj_loaded, 16)
            e.dma_start(p_in, t["p"][0, 0].rearrange("(i p) n -> p i n", p=P)).then_inc(p_loaded, 16)

            for i in range(TILES):
                e.wait_ge(x_ready, i + 1)
                nc.scalar.activation(xn[:, i, :], x[:, i, :], ACT.Square,
                                     accum_out=ss[:, i:i + 1]).then_inc(ss_ready, 1)
            e.wait_ge(exp_in, 1)
            for i in range(TILES):
                nc.scalar.activation(expo[:, i, :], logit[:, i, 0:N_EXPERTS], ACT.Exp,
                                     bias=neg[:, i:i + 1]).then_inc(exp_ready, 1)

            def sigmoid(s, qi):
                e.wait_ge(s.gate_ready, qi + 1)
                nc.scalar.activation(sig, gate, ACT.Sigmoid, scale=ALPHA).then_inc(s.sig_ready, 1)

            def read_rows(s, pair):
                e.wait_ge(s.xposed, pair + 1)
                nc.scalar.copy(slot_rows, two_banks(5)).then_inc(s.os_ready, 1)

            def read_down(s, pair):
                e.wait_ge(s.chunk_used, s.base + 24 * pair + 24)
                nc.scalar.copy(dT, two_banks(2)).then_inc(s.dT_ready, 1)

            sigmoid(first, 0)
            e.wait_ge(pT_psum, 1)
            nc.scalar.copy(pT, bank_cols(5, 2)).then_inc(pT_ready, 1)
            sigmoid(first, 1)
            read_down(first, 0)
            with e.Fori(1, PAIRS) as pair:
                sigmoid(first, 2 * pair)
                read_rows(first, pair - 1)
                sigmoid(first, 2 * pair + 1)
                read_down(first, pair)
            read_rows(first, PAIRS - 1)

            def body(j, ex, low):
                sigmoid(more, 2 * j)
                sigmoid(more, 2 * j + 1)
                read_down(more, j)
                read_rows(more, j)
                e.wait_ge(more.pair_done, j + 1)

            def skipped():
                for s, n in ((more.sig_ready, 2), (more.dT_ready, 1), (more.os_ready, 1)):
                    e.sem_inc(s, n)

            more_pairs("act", e, body, skipped)
            e.wait_ge(x_ready, 2 * TILES)
            for i in range(TILES):
                nc.scalar.activation(xn[:, i, :], x[:, i, :], ACT.Square,
                                     accum_out=ss[:, i:i + 1]).then_inc(ss_ready, 1)
            for n in range(2):
                e.wait_ge(used, PLE_CHUNK + 2 * n + 2)
                if n:
                    e.wait_ge(x_ready, 3 * TILES)
                for i in range(TILES):
                    nc.scalar.activation(ple_gate[:, i, :], ps[:, 2 * n + i, :], ACT.Sigmoid).then_inc(gate_sig, 1)
            for i in range(TILES):
                e.wait_ge(x_ready, 3 * TILES + i + 1)
                nc.scalar.activation(xn[:, i, :], x[:, i, :], ACT.Square,
                                     accum_out=ss[:, i:i + 1]).then_inc(ss_ready, 1)

        @block.vector
        def _(dve):
            ve = nc.vector
            counts_of = {}

            order = [vec_order]

            def step(ins, s=None):
                s = s or order[0]
                c = counts_of.setdefault(id(s), Count())
                ins.then_inc(s, 1)
                c.n += 1
                dve.wait_ge(s, c.value())

            def own(s):
                return counts_of.setdefault(id(s), Count())

            dve.wait_ge(vec_loaded, 16 * 6)
            step(ve.tensor_copy(pos_row, pos_int), pos_cast)
            dve.wait_ge(vec_psum, 1)
            step(ve.tensor_copy(vecs[:, :], ps[:, 0, 0:5 * KD]))
            step(ve.tensor_copy(pos, ps[:, 0, 64:64 + TILES]), vecs_read)

            def normalise(n):
                dve.wait_ge(rstd_ready, (1, 3, 4)[n])
                for i in range(TILES):
                    step(ve.tensor_scalar(xn[:, i, :], x[:, i, :], rstd[:, i:i + 1], None, ALU.mult), xn_ready)
                g = (G_MIX, G_FFN, G_PLE)[n]
                for j in range(4):
                    dve.wait_ge(xT_psum, 4 * n + j + 1)
                    step(ve.tensor_tensor(hT[:, 2 * j:2 * j + 2, :], bank_cols(4 + j, 2),
                                          across(vecs[:, g + 2 * j:g + 2 * j + 2], SEQ), ALU.mult), hT_ready)

            normalise(0)
            for i in range(TILES):
                step(ve.tensor_scalar(cos[:, i, :], const[:, INVF:INVF + 64], pos[:, i:i + 1], None, ALU.mult))
            for dst, shift in ((angle, 0.0), (turns, 0.25)):
                step(ve.tensor_scalar(nsin, cos, 1.0 / 6.283185307179586, shift, ALU.mult, ALU.add))
                step(ve.tensor_scalar(nsin, nsin, ROUND, None, ALU.add))
                step(ve.tensor_scalar(nsin, nsin, ROUND, None, ALU.subtract))
                step(ve.scalar_tensor_tensor(dst, nsin, -TWO_PI_HI, cos, ALU.mult, ALU.add))
                step(ve.scalar_tensor_tensor(dst, nsin, -TWO_PI_MID, dst, ALU.mult, ALU.add))
                step(ve.scalar_tensor_tensor(dst, nsin, -TWO_PI_LO, dst, ALU.mult, ALU.add))
                if shift:
                    step(ve.tensor_scalar(dst, dst, 1.5707963267948966, None, ALU.add))
                last = ve.tensor_scalar(dst, dst, 3.1415925, -3.1415925, ALU.min, ALU.max)
                step(last, angles_ready if shift else None)
            dve.wait_ge(sin_ready, 2)
            step(ve.tensor_scalar(nsin, sin, -1.0, None, ALU.mult))

            def heads4(ap):
                return ap.rearrange("p (h x f) -> p h x f", h=4, x=2)

            def per_head(ap, n):
                return ap.unsqueeze(1).to_broadcast([P, n, 64])

            for j in range(4):
                n, dst = j % 2, (q if j < 2 else k)
                dve.wait_ge(used, block_chunk(j) + 2)
                for i in range(TILES):
                    src = heads4(ps[:, 2 * n + i, :])
                    step(ve.tensor_tensor(rot_a.rearrange("p (h f) -> p h f", f=64),
                                          ps[:, 2 * n + i, :].rearrange("p (h f) -> p h f", f=64),
                                          per_head(cos[:, i, :], 8), ALU.mult))
                    step(ve.tensor_tensor(heads4(rot_b)[:, :, 0, :], src[:, :, 1, :], per_head(nsin[:, i, :], 4), ALU.mult))
                    step(ve.tensor_tensor(heads4(rot_b)[:, :, 1, :], src[:, :, 0, :], per_head(sin[:, i, :], 4), ALU.mult), read_dve)
                    step(ve.tensor_tensor(dst[:, i, n * N:(n + 1) * N], rot_a, rot_b, ALU.add), rotated)
            dve.wait_ge(const_loaded, 16)
            dve.wait_ge(qkT_psum, 8)
            k0 = k[:, 0, :].rearrange("p (h f) -> p h f", f=P)
            step(ve.tensor_tensor(k0, k0, across(const[:, ZETA:ZETA + HEADS], P), ALU.mult), kz_ready)

            def decay_scores(g):
                for c in range(TILES):
                    dve.wait_ge(ret_psum, 5 * g + c + 1)
                    step(ve.tensor_tensor(scoresT[:, c, 0:N], ps[:, 4 + c, :],
                                          const[:, DMAT + g * N:DMAT + (g + 1) * N], ALU.mult), scores_ready)

            def read_ret(g):
                dve.wait_ge(ret_psum, 5 * g + 4)
                step(ve.tensor_copy(ret[:, 0, g * N:(g + 1) * N], ps[:, 4, :]))
                dve.wait_ge(ret_psum, 5 * g + 5)
                step(ve.tensor_tensor(cross.rearrange("p (h f) -> p h f", f=P), bank_cols(7, 4),
                                      across(const[:, XI + 4 * g:XI + 4 * g + 4], P), ALU.mult))
                step(ve.tensor_tensor(ret[:, 1, g * N:(g + 1) * N], cross, ps[:, 5, :], ALU.add), ret_read)

            def silu(j):
                n = j % 2
                for i in range(TILES):
                    dve.wait_ge(sig_g, 2 * (j - 8) + i + 1)
                    z = silu_g[:, i, n * N:(n + 1) * N]
                    step(ve.tensor_tensor(z, z, ps[:, 2 * n + i, :], ALU.mult), read_dve)

            decay_scores(0)
            read_ret(0)
            silu(8)
            decay_scores(1)
            silu(9)
            read_ret(1)
            flat = [z.rearrange("p t (h f) -> p (t h) f", f=P) for z in (ret, square)]
            step(ve.tensor_reduce(mean, flat[0], AX.X, ALU.add))
            step(ve.tensor_scalar(mean, mean, 1.0 / P, None, ALU.mult))
            step(ve.tensor_tensor(flat[0], flat[0], across(mean, P), ALU.subtract), square_in)
            dve.wait_ge(squared, 1)
            step(ve.tensor_reduce(var, flat[1], AX.X, ALU.add), var_ready)
            dve.wait_ge(rstd_ready, 2)
            step(ve.tensor_tensor(flat[0], flat[0], across(var, P), ALU.mult))
            step(ve.tensor_tensor(ret, ret, silu_g, ALU.mult), yret_ready)
            dve.wait_ge(used, POOL_CHUNK + 1)
            for j in range(4):
                step(ve.tensor_tensor(ypoolT[:, 2 * j:2 * j + 2, :], bank_cols(4 + j, 2),
                                      across(vecs[:, G_POOL + 2 * j:G_POOL + 2 * j + 2], SEQ), ALU.mult), ypT_ready)
            for j in range(4):
                dve.wait_ge(yrT_psum, j + 1)
                step(ve.tensor_tensor(yretT[:, 2 * j:2 * j + 2, :], bank_cols(4 + j, 2),
                                      across(vecs[:, G_RET + 2 * j:G_RET + 2 * j + 2], SEQ), ALU.mult), yrT_ready)
            dve.wait_ge(read_act, 2 * 8)
            for unit in range(4):
                n, is_a = unit // 2, unit % 2
                dve.wait_ge(used, BRANCH_CHUNK + 2 * unit + 2)
                for i in range(TILES):
                    m = merged[:, i, n * N:(n + 1) * N]
                    g = gates[1 - is_a][:, i, n * N:(n + 1) * N]
                    final = branch_read if i == TILES - 1 else None
                    if is_a:
                        step(ve.tensor_tensor(branch_tmp, g, ps[:, 2 + i, :], ALU.mult))
                        step(ve.tensor_tensor(m, m, branch_tmp, ALU.add), final)
                    else:
                        step(ve.tensor_tensor(m, g, ps[:, i, :], ALU.mult), final)
            for n in range(2):
                dve.wait_ge(used, OUT_CHUNK + 2 * n + 2)
                for i in range(TILES):
                    z = x[:, i, n * N:(n + 1) * N]
                    step(ve.tensor_tensor(z, z, ps[:, 2 * n + i, :], ALU.add), x_ready if n else None)
            normalise(1)
            dve.wait_ge(route_psum, 1)
            step(ve.tensor_copy(bgu, ps[:, 3, :].rearrange("p (m e) -> p e m", e=N_EXPERTS)))
            dve.wait_ge(logits_psum, 1)
            step(ve.memset(logit[:, :, N_EXPERTS:], BIG))
            step(ve.tensor_copy(logit[:, :, 0:N_EXPERTS], ps[:, 0, 0:TILES * N_EXPERTS].rearrange("p (t e) -> p t e", t=TILES)))
            for i in range(TILES):
                step(ve.max(top[:, i, :], logit[:, i, 0:N_EXPERTS]))
            step(ve.tensor_scalar(neg.unsqueeze(2), top[:, :, 0:1], -1.0, None, ALU.mult), exp_in)
            step(ve.memset(top[:, :, TOP_K:8], BIG))
            for i in range(TILES):
                step(ve.match_replace(marked[:, i, :], top[:, i, :], logit[:, i, :], -BIG))
            step(ve.tensor_scalar(mask, marked[:, :, 0:N_EXPERTS], -BIG, None, ALU.is_equal), mask_ready)
            dve.wait_ge(exp_ready, TILES)
            step(ve.memset(comb[:, :, N_EXPERTS:], 0.0))
            step(ve.memset(rank[:, :, N_EXPERTS:], -1.0))
            step(ve.tensor_tensor(expo, expo, mask, ALU.mult))
            step(ve.tensor_reduce(tot, expo, AX.X, ALU.add))
            step(ve.reciprocal(tot, tot))
            step(ve.tensor_tensor(comb[:, :, 0:N_EXPERTS], expo, across(tot, N_EXPERTS), ALU.mult), comb_ready)
            dve.wait_ge(route_psum, 2)
            r = rank[:, :, 0:N_EXPERTS]
            step(ve.scalar_tensor_tensor(r, ps[:, 1, 0:TILES * N_EXPERTS].rearrange("p (t e) -> p t e", t=TILES), 1.0,
                                         mask, ALU.add, ALU.mult))
            step(ve.tensor_scalar(r, r, 1.0, None, ALU.subtract))
            step(ve.tensor_copy(count_f, ps[0:1, 1, 2 * N_EXPERTS:3 * N_EXPERTS]))
            step(ve.tensor_copy(counts, count_f))
            step(ve.tensor_reduce(count_top_f, count_f, AX.X, ALU.max))
            step(ve.tensor_copy(count_top, count_top_f))
            dve.wait_ge(route_psum, 3)
            dve.wait_ge(late_loaded, 32)
            step(ve.tensor_copy(combT, ps[0:N_EXPERTS, 2, 0:SEQ]), route_ready)

            def make_onehot(s, par, e, low=0):
                for i in range(TILES):
                    step(ve.tensor_scalar(onehot[par][:, i, :], const[:, IOTA + low:IOTA + low + BLOCK],
                                          rank[:, i, bass.ds(e, 1)], None, ALU.is_equal),
                         s.onehot_ready if i == TILES - 1 else None)

            def make_weighted(s, experts, lows):
                for h, (e, low) in enumerate(zip(experts, lows)):
                    for i in range(TILES):
                        last = h == 1 and i == TILES - 1
                        step(ve.tensor_scalar(weighted[:, i, h * BLOCK:(h + 1) * BLOCK],
                                              const[:, IOTA + low:IOTA + low + BLOCK],
                                              rank[:, i, bass.ds(e, 1)], comb[:, i, bass.ds(e, 1)],
                                              ALU.is_equal, ALU.mult), s.sw_ready if last else None)

            def read_gather(s, qi, par):
                dve.wait_ge(s.gathered, qi + 1)
                step(ve.tensor_tensor(hg[par], bank_cols(4), across(vecs[:, G_FFN:G_FFN + KD], BLOCK), ALU.mult), s.hg_ready)

            def activate(s, pair, h, e):
                qi = 2 * pair + h
                dve.wait_ge(s.chunk_used, s.base + PER_EXPERT * qi + UP_CHUNKS)
                bias = bgu[:, bass.ds(e, 1), :].rearrange("p e m -> p (e m)")
                step(ve.tensor_tensor(gate, bank_cols(0), across(bias[:, 0:KD], BLOCK), ALU.add))
                step(ve.tensor_scalar(gate, gate, LIMIT, None, ALU.min), s.gate_ready)
                step(ve.tensor_tensor(up, bank_cols(1), across(bias[:, KD:2 * KD], BLOCK), ALU.add))
                step(ve.tensor_scalar(up, up, LIMIT, -LIMIT, ALU.min, ALU.max))
                step(ve.scalar_tensor_tensor(prod, up, 1.0, gate, ALU.add, ALU.mult))
                dve.wait_ge(s.sig_ready, qi + 1)
                step(ve.tensor_tensor(act, prod, sig, ALU.mult), s.act_ready)

            def read_weights(s, pair):
                dve.wait_ge(s.swt_done, pair + 1)
                step(ve.tensor_copy(scatterT, ps[:, 7, 0:SEQ]), s.st_ready)

            def accumulate(s, pair):
                for i in range(4):
                    dve.wait_ge(s.scattered, 4 * pair + i + 1)
                    tile, n = i // 2, i % 2
                    z = x[:, tile, n * N:(n + 1) * N]
                    step(ve.tensor_tensor(z, z, ps[:, (7, 5, 6, 7)[i], :], ALU.add), s.acc_done)

            def pair_steps(pair, is_first=False):
                make_onehot(first, 1, 2 * pair + 1)
                activate(first, pair, 0, 2 * pair)
                read_gather(first, 2 * pair + 1, 1)
                if is_first:
                    for i in range(4):
                        dve.wait_ge(ple_psum, i + 1)
                        tile, n = i // 2, i % 2
                        step(ve.tensor_copy(ple[:, tile, n * N:(n + 1) * N], ps[:, (7, 5, 6, 7)[i], :]), first.acc_done)
                else:
                    accumulate(first, pair - 1)
                make_weighted(first, (2 * pair, 2 * pair + 1), (0, 0))
                make_onehot(first, 0, 2 * pair + 2)
                activate(first, pair, 1, 2 * pair + 1)
                read_gather(first, 2 * pair + 2, 0)
                read_weights(first, pair)

            make_onehot(first, 0, 0)
            read_gather(first, 0, 0)
            for i in range(4):
                dve.wait_ge(bias_psum, i + 1)
                tile, n = i // 2, i % 2
                z = x[:, tile, n * N:(n + 1) * N]
                step(ve.tensor_tensor(z, z, ps[:, (0, 1, 5, 6)[i], :], ALU.add), bias_read)
            pair_steps(0, True)
            per_turn = {vec_order: 2 * 1 + 2 * 4 + 3, first.onehot_ready: 2, first.gate_ready: 2, first.act_ready: 2,
                        first.hg_ready: 2, first.acc_done: 4, first.sw_ready: 1, first.st_ready: 1}
            with dve.Fori(1, PAIRS) as pair:
                for s, n in per_turn.items():
                    own(s).enter(pair - 1, n)
                pair_steps(pair)
                for s in per_turn:
                    own(s).leave(PAIRS - 1)
            accumulate(first, PAIRS - 1)

            more_turn = {more.onehot_ready: 2, more.gate_ready: 2, more.act_ready: 2, more.hg_ready: 2,
                         more.acc_done: 4, more.sw_ready: 1, more.st_ready: 1,
                         more.order: 2 * 1 + 2 * 4 + 3}

            def body(j, e, low):
                for s, n in more_turn.items():
                    own(s).n, own(s).base = 0, j * n
                make_onehot(more, 0, e, low)
                read_gather(more, 2 * j, 0)
                make_onehot(more, 1, e, low + BLOCK)
                activate(more, j, 0, e)
                read_gather(more, 2 * j + 1, 1)
                make_weighted(more, (e, e), (low, low + BLOCK))
                activate(more, j, 1, e)
                read_weights(more, j)
                accumulate(more, j)
                dve.sem_inc(more.pair_done, 1)
                for s, n in more_turn.items():
                    assert own(s).n == n, (s, own(s).n, n)

            def skipped():
                for s, n in more_turn.items():
                    dve.sem_inc(s, n)
                dve.sem_inc(more.pair_done, 1)

            order[0] = more.order
            more_pairs("dve", dve, body, skipped)
            order[0] = vec_order

            dve.sem_inc(x_ready, TILES)
            own(x_ready).n += TILES
            normalise(2)
            for n in range(2):
                for i in range(TILES):
                    dve.wait_ge(gate_sig, 2 * n + i + 1)
                    z = x[:, i, n * N:(n + 1) * N]
                    g = ple_gate[:, i, :]
                    step(ve.tensor_tensor(g, g, ple[:, i, n * N:(n + 1) * N], ALU.mult))
                    step(ve.tensor_tensor(z, z, g, ALU.add), x_ready)
            dve.wait_ge(rstd_ready, 5)
            for i in range(TILES):
                step(ve.scalar_tensor_tensor(result[:, i, :], x[:, i, :], rstd[:, i:i + 1], g_final,
                                             ALU.mult, ALU.mult), out_ready)


def constants():
    import numpy as np
    c = np.zeros((P, N_CONST), np.float32)
    r = np.arange(P)
    c[:, IDENT:IDENT + P] = np.eye(P)
    c[:, INVF:INVF + 64] = np.power(np.float32(10000.0), -(np.arange(64, dtype=np.float32) / np.float32(64)))
    c[:, TRI:TRI + P] = r[:, None] < r[None, :]
    c[:, ONES:ONES + P] = 1.0
    c[:, IOTA:DMAT] = np.arange(DMAT - IOTA)
    scale = float(P) ** -0.5
    log_gamma = np.log1p(-np.exp2(-5.0 - np.arange(HEADS)))
    for h in range(HEADS):
        d = r[None, :] - r[:, None]
        c[:, DMAT + h * P:DMAT + (h + 1) * P] = np.where(d >= 0, np.exp(log_gamma[h] * np.maximum(d, 0)) * scale, 0)
        c[:, ZETA + h] = np.exp(log_gamma[h] * (P - 1 - r)) * scale
        c[:, XI + h] = np.exp(log_gamma[h] * (r + 1))
    pos = np.arange(SEQ)
    for i, w in enumerate(WINDOWS):
        lag = pos[None, :] - pos[:, None]
        m = ((lag >= 0) & (lag < w)) / np.minimum(pos + 1, w)[None, :] - np.eye(SEQ)
        at = POOLM + 3 * P * i
        c[:, at:at + P], c[:, at + P:at + 2 * P], c[:, at + 2 * P:at + 3 * P] = m[:P, :P], m[:P, P:], m[P:, P:]
    return c


_INS = ["x", "p", "positions", "g_mix_norm", "w_in", "g_ret_norm", "w_pool", "pool_scale", "w_branch", "w_out",
        "g_ffn_norm", "w_router", "b_router", "w_gate_up", "b_gate_up", "w_down", "b_down", "g_ple_norm",
        "w_ple_gate", "w_ple_proj", "g_final"]


def kernel(**inputs):
    import numpy as np
    import concourse.bacc as bacc
    from concourse.bass_utils import run_bass_kernel_spmd

    nc = bacc.Bacc("TRN2", target_bir_lowering=False, num_devices=1)
    arrays = {f"in_{n}": np.ascontiguousarray(inputs[n]) for n in _INS}
    arrays["in_const"] = constants()
    tensors = {n[3:]: nc.dram_tensor(n, a.shape, mybir.dt.from_np(a.dtype), kind="ExternalInput").ap()
               for n, a in arrays.items()}
    tensors["y"] = nc.dram_tensor("out_y", (1, SEQ, D), F32, kind="ExternalOutput").ap()
    build(nc, tensors)
    return run_bass_kernel_spmd(nc, [arrays], core_ids=[0]).results[0]["out_y"]
```

```python
from contextlib import ExitStack

import concourse.bass as bass
from concourse import mybir

F32 = mybir.dt.float32
I32 = mybir.dt.int32
ALU = mybir.AluOpType
ACT = mybir.ActivationFunctionType
AX = mybir.AxisListType

P = 128
SEQ, D = 256, 1024
TILES = SEQ // P
KD = D // P
HEADS = 8
N_EXPERTS, TOP_K = 32, 4
FF = 1024
PLE = 256
WINDOWS = (2, 4, 8, 16)
BLOCK = 64
BLOCKS_MAX = SEQ // BLOCK
RMS_EPS, GN_EPS = 1e-6, 1e-5
LIMIT, ALPHA = 7.0, 1.702
BIG = 3.0e38
TWO_PI_HI, TWO_PI_MID = 6.28125, 0.0019350051879882812
TWO_PI_LO = 6.283185307179586 - TWO_PI_HI - TWO_PI_MID
ROUND = 12582912.0

SLOTS, SLOT = 12, 2048
N = 512
Q, K_, V_, U, G_, GA, GB = range(7)
COLUMN_BLOCKS = [0, 1, 2, 3, 4, 5, 8, 9, 6, 7, 10, 11, 12, 13]
POOL_AFTER = 12


def block_chunk(j):
    return 2 * j + (j >= POOL_AFTER)


POOL_CHUNK = 2 * POOL_AFTER
BRANCH_CHUNK = 2 * len(COLUMN_BLOCKS) + 1
OUT_CHUNK = BRANCH_CHUNK + 8
EXPERT_CHUNK = OUT_CHUNK + 4
UP_CHUNKS, DOWN_CHUNKS = 8, 4
PER_EXPERT = UP_CHUNKS + DOWN_CHUNKS
PER_PAIR = 2 * PER_EXPERT
PAIRS = N_EXPERTS // 2
PLE_CHUNK = EXPERT_CHUNK + N_EXPERTS * PER_EXPERT

IDENT, INVF = 0, P
EARLY = INVF + 64
TRI = EARLY
ONES = TRI + P
IOTA = ONES + P
DMAT = IOTA + BLOCKS_MAX * BLOCK + BLOCK
ZETA = DMAT + HEADS * P
XI = ZETA + HEADS
SEL = XI + HEADS
POOLM = SEL + P
N_CONST = POOLM + 3 * len(WINDOWS) * P

G_MIX, G_RET, G_POOL, G_FFN, G_PLE = (KD * i for i in range(5))


class ExpertSemaphores:

    def __init__(self, sem, tag, base, acc0):
        self.base, self.acc0 = base, acc0
        self.onehot_ready = sem(tag + "_onehot_ready")
        self.gathered = sem(tag + "_gathered")
        self.hg_ready = sem(tag + "_hg_ready")
        self.bias_loaded = sem(tag + "_bias_loaded")
        self.up_done = sem(tag + "_up_done")
        self.gate_ready = sem(tag + "_gate_ready")
        self.up_read = sem(tag + "_up_read")
        self.sig_ready = sem(tag + "_sig_ready")
        self.act_ready = sem(tag + "_act_ready")
        self.act_xposed = sem(tag + "_act_xposed")
        self.actT_ready = sem(tag + "_actT_ready")
        self.os_ready = sem(tag + "_os_ready")
        self.sw_ready = sem(tag + "_sw_ready")
        self.swt_done = sem(tag + "_swt_done")
        self.st_ready = sem(tag + "_st_ready")
        self.scattered = sem(tag + "_scattered")
        self.acc_done = sem(tag + "_acc_done")
        self.chunk_used = sem(tag + "_chunk_used")
        self.pair_done = sem(tag + "_pair_done")
        self.order = sem(tag + "_order")
        self.loaded = [sem(f"{tag}_loaded{i}") for i in range(SLOTS)]


class Count:

    def __init__(self):
        self.n, self.base = 0, 0

    def enter(self, turns_before, per_turn):
        self.start, self.per_turn, self.before = self.n, per_turn, self.n
        self.base, self.n = turns_before * per_turn, self.n

    def leave(self, turns):
        assert self.n - self.before == self.per_turn, (self.n - self.before, self.per_turn)
        self.base, self.n = 0, self.before + turns * self.per_turn

    def value(self):
        return self.base + self.n


def build(nc, t):
    ctx = ExitStack()
    with ctx:
        def sb(name, shape, dt=F32):
            return ctx.enter_context(nc.sbuf_tensor(name, shape, dt))

        def sem(name):
            return ctx.enter_context(nc.semaphore(name))

        ring = sb("ring", [P, SLOTS, SLOT])
        x = sb("x", [P, TILES, D])
        xn = sb("xn", [P, TILES, D])
        hT = sb("hT", [P, KD, SEQ])
        B = [sb(f"B{i}", [P, 2048]) for i in range(9)]
        const = sb("const", [P, N_CONST])
        vecs = sb("vecs", [P, 5 * KD])
        small = sb("small", [P, 64])
        ps = ctx.enter_context(nc.psum_tensor("ps", [P, 8, N], F32))

        ident = const[:, IDENT:IDENT + P]
        tri = const[:, TRI:TRI + P]
        ones = const[:, ONES:ONES + P]

        def rows(buf, width=D):
            return buf[:, 0:TILES * width].rearrange("p (t n) -> p t n", t=TILES)

        def cols(buf):
            return buf[:, :].rearrange("p (k s) -> p k s", k=KD)

        q, ret = rows(B[0]), rows(B[0])
        k = rows(B[1])
        scoresT = B[1][:, D:2 * D].rearrange("p (c n) -> p c n", c=TILES)
        square, merged = rows(B[1]), rows(B[1])
        v, mixedT = rows(B[2]), cols(B[2])
        qT, yretT = cols(B[3]), cols(B[3])
        kT, ypoolT = cols(B[4]), cols(B[4])
        rot_a, rot_b = B[4][:, 0:N], B[4][:, N:2 * N]
        silu_g, mergedT = rows(B[5]), cols(B[5])
        kv, cross = B[6][:, 0:N], B[6][:, N:2 * N]
        gates = [rows(B[6]), rows(B[7])]
        u = rows(B[8])
        branch_tmp = B[0][:, 0:N]
        vec_rows = B[6][0:5 * KD, 0:P]
        pos_int = B[6][0:TILES, P:2 * P].bitcast(I32)
        pos_row = B[6][0:TILES, 2 * P:3 * P]
        angle = B[7][:, 0:P].rearrange("p (t f) -> p t f", t=TILES)
        turns = B[7][:, P:2 * P].rearrange("p (t f) -> p t f", t=TILES)
        cos = B[8][:, 2 * P:3 * P].rearrange("p (t f) -> p t f", t=TILES)
        sin = B[8][:, 3 * P:4 * P].rearrange("p (t f) -> p t f", t=TILES)
        nsin = B[8][:, 4 * P:5 * P].rearrange("p (t f) -> p t f", t=TILES)
        waste = B[8][:, D:2 * D]
        hg = B[0][:, 0:D].rearrange("p (k s) -> p k s", k=KD)
        gate, up, sig = B[0][:, D:2 * D], B[1][:, 0:D], B[1][:, D:2 * D]
        bias_rows = B[5][0:2, :]
        actT = B[2][:, 0:D].rearrange("p (k s) -> p k s", k=KD)
        slot_rows = B[2][:, D:2 * D]
        scatterT = B[3][:, 0:SEQ]
        onehot, weighted = (B[3][:, i:i + SEQ].rearrange("p (t s) -> p t s", t=TILES) for i in (256, 512))
        p_in = B[3][:, 768:1280].rearrange("p (t n) -> p t n", t=TILES)
        pT = B[3][:, 1280:1792].rearrange("p (c s) -> p c s", c=2)
        EP = N_EXPERTS + 2
        at = [0]

        def piece(n):
            at[0] += n
            return B[4][:, at[0] - n:at[0]]

        combT = piece(SEQ)[0:N_EXPERTS, :]
        rank = piece(TILES * EP).rearrange("p (t e) -> p t e", t=TILES)
        comb = piece(TILES * EP).rearrange("p (t e) -> p t e", t=TILES)
        logit = piece(TILES * 36).rearrange("p (t e) -> p t e", t=TILES)
        marked = piece(TILES * 36).rearrange("p (t e) -> p t e", t=TILES)
        top = piece(TILES * 8).rearrange("p (t e) -> p t e", t=TILES)
        mask = piece(TILES * N_EXPERTS).rearrange("p (t e) -> p t e", t=TILES)
        expo = piece(TILES * N_EXPERTS).rearrange("p (t e) -> p t e", t=TILES)
        counts = piece(N_EXPERTS)[0:1, :].bitcast(I32)
        count_f = piece(N_EXPERTS)[0:1, :]
        count_top = piece(1)[0:1, :].bitcast(I32)
        count_top_f = piece(1)[0:1, :]
        w_router = piece(KD * N_EXPERTS).rearrange("p (k e) -> p k e", k=KD)
        b_router = piece(N_EXPERTS)[0:1, :]
        assert at[0] <= 2048
        w_proj = B[6][:, :].rearrange("p (c n) -> p c n", c=2)
        ple = rows(B[7])
        b_down = B[8][0:N_EXPERTS, 0:D]
        g_final = B[8][:, D:2 * D]
        result = rows(B[0])
        ple_gate = B[1][:, 0:2 * N].rearrange("p (t n) -> p t n", t=TILES)

        pos, ss, rstd, neg, tot = (small[:, 2 * i:2 * i + 2] for i in range(5))
        mean, var, exponent = (small[:, i:i + 16] for i in (16, 32, 48))

        x_loaded, vec_loaded, early_loaded, const_loaded = map(sem, ("x_loaded", "vec_loaded", "early_loaded", "const_loaded"))
        router_loaded, late_loaded = sem("router_loaded"), sem("late_loaded")
        p_loaded, proj_loaded, stored = map(sem, ("p_loaded", "proj_loaded", "stored"))
        vec_order = sem("vec_order")
        pos_cast, vec_psum, vecs_read = map(sem, ("pos_cast", "vec_psum", "vecs_read"))
        angles_ready, sin_ready = sem("angles_ready"), sem("sin_ready")
        ss_ready, xn_ready, xT_psum, hT_ready = map(sem, ("ss_ready", "xn_ready", "xT_psum", "hT_ready"))
        var_ready, mean_square, rstd_ready = sem("var_ready"), sem("mean_square"), sem("rstd_ready")
        read_dve, read_act = sem("read_dve"), sem("read_act")
        rotated, qkT_psum, qkT_ready, kz_ready = map(sem, ("rotated", "qkT_psum", "qkT_ready", "kz_ready"))
        ret_psum, scores_ready, kv_ready, ret_read = map(sem, ("ret_psum", "scores_ready", "kv_ready", "ret_read"))
        square_in, squared, sig_g = sem("square_in"), sem("squared"), sem("sig_g")
        pool_psum, mixT_ready, ypT_ready = map(sem, ("pool_psum", "mixT_ready", "ypT_ready"))
        yret_ready, yrT_psum, yrT_ready = map(sem, ("yret_ready", "yrT_psum", "yrT_ready"))
        branch_read, mT_psum, mT_ready, x_ready = map(sem, ("branch_read", "mT_psum", "mT_ready", "x_ready"))
        logits_psum, exp_in, exp_ready = map(sem, ("logits_psum", "exp_in", "exp_ready"))
        mask_ready, comb_ready, route_psum, route_ready = map(sem, ("mask_ready", "comb_ready", "route_psum", "route_ready"))
        bias_psum, bias_read = sem("bias_psum"), sem("bias_read")
        pT_psum, pT_ready, ple_psum = sem("pT_psum"), sem("pT_ready"), sem("ple_psum")
        gate_sig, out_ready = sem("gate_sig"), sem("out_ready")

        first = ExpertSemaphores(sem, "first", EXPERT_CHUNK, 4)
        more = ExpertSemaphores(sem, "more", 0, 0)
        used, loaded = first.chunk_used, first.loaded

        block = ctx.enter_context(nc.Block())

        def two_banks(b):
            return ps[:, b:b + 2, :].rearrange("p b n -> p (b n)")

        def bank_cols(b, n=KD):
            return ps[:, b, :].rearrange("p (k s) -> p k s", k=n)

        SUM_BANKS = (6, 7, 4, 5)

        def across(ap, n):
            return ap.unsqueeze(2).to_broadcast([P, ap.shape[1], n])

        def block_read(j):
            dve_blocks = [0, 1, 2, 3, 8, 9]
            if j in dve_blocks:
                return read_dve, 2 * (dve_blocks.index(j) + 1)
            act_blocks = [4, 5, 6, 7, 10, 11, 12, 13]
            return read_act, 2 * (act_blocks.index(j) + 1)

        def slot_of(c):
            return c % SLOTS

        def chunk_ready(eng, c):
            eng.wait_ge(loaded[slot_of(c)], 16 * (c // SLOTS + 1))

        def expert_ready(eng, s, pair, h, i):
            c = s.base + 2 * i + h
            eng.wait_ge(s.loaded[slot_of(c)], 16 * (c // SLOTS + 1) + 32 * pair)

        left_body = {n: sem(f"left_body_{n}") for n in ("sp", "pe", "act", "dve")}

        def more_pairs(name, eng, body, skipped):
            top_count = eng.value_load(count_top[0:1, 0:1], min_val=0, max_val=SEQ)
            with eng.If(top_count > BLOCK):
                with eng.Fori(0, N_EXPERTS) as e:
                    for half in range(2):
                        low = (1 + 2 * half) * BLOCK
                        n_tokens = eng.value_load(counts[0:1, bass.ds(e, 1)], min_val=0, max_val=SEQ)
                        with eng.If(n_tokens > low):
                            body(2 * e + half, e, low)
                            eng.sem_inc(left_body[name], 1)
                        with eng.Else():
                            skipped()
                        eng.nop()
                eng.nop()
            eng.nop()

        @block.sync
        def _(sp):
            def load(c, src, shape=None):
                if c >= SLOTS:
                    sp.wait_ge(used, c - SLOTS + 1)
                dst = ring[:, slot_of(c), :]
                if shape:
                    dst = dst.rearrange("p (k n) -> p k n", k=shape)
                sp.dma_start(dst, src).then_inc(loaded[slot_of(c)], 16)

            w_in = t["w_in"][0].rearrange("(k p) n -> p k n", p=P)
            for j, cb in enumerate(COLUMN_BLOCKS):
                if j == POOL_AFTER:
                    load(POOL_CHUNK, t["w_pool"][0].rearrange("g (k p) n -> p (g k) n", p=P), 8)
                for half in range(2):
                    load(block_chunk(j) + half, w_in[:, 4 * half:4 * half + 4, cb * N:(cb + 1) * N], 4)
            for unit in range(4):
                w = t["w_branch"][0, 1 - unit % 2].rearrange("(k p) n -> p k n", p=P)
                for half in range(2):
                    load(BRANCH_CHUNK + 2 * unit + half,
                         w[:, 4 * half:4 * half + 4, (unit // 2) * N:(unit // 2 + 1) * N], 4)
            w_out = t["w_out"][0].rearrange("(k p) n -> p k n", p=P)
            for n in range(2):
                for half in range(2):
                    load(OUT_CHUNK + 2 * n + half, w_out[:, 4 * half:4 * half + 4, n * N:(n + 1) * N], 4)

            def load_pair(s, pair, experts):
                for i in range(PER_EXPERT):
                    for h, e in enumerate(experts):
                        c = s.base + 2 * i + h
                        if c >= SLOTS:
                            sp.wait_ge(s.chunk_used, PER_PAIR * pair + c - SLOTS + 1)
                        dst = ring[:, slot_of(c), :]
                        if i < UP_CHUNKS:
                            src = t["w_gate_up"][0, bass.ds(e, 1), i * P:(i + 1) * P, :].rearrange("e p n -> p (e n)")
                        else:
                            r = (i - UP_CHUNKS) * 2 * P
                            src = t["w_down"][0, bass.ds(e, 1), r:r + 2 * P, :].rearrange("e (k p) n -> p (e k) n", p=P)
                            dst = dst.rearrange("p (k n) -> p k n", k=2)
                        sp.dma_start(dst, src).then_inc(s.loaded[slot_of(c)], 16)

            with sp.Fori(0, PAIRS) as pair:
                load_pair(first, pair, (2 * pair, 2 * pair + 1))

            def body(j, e, low):
                load_pair(more, j, (e, e))
                sp.wait_ge(more.pair_done, j + 1)

            def skipped():
                for s in range(SLOTS):
                    sp.sem_inc(more.loaded[s], 32)

            sp.wait_ge(route_ready, 1)
            sp.wait_ge(used, PLE_CHUNK)
            more_pairs("sp", sp, body, skipped)
            w_gate = t["w_ple_gate"][0].rearrange("(k p) n -> p k n", p=P)
            for n in range(2):
                for half in range(2):
                    load(PLE_CHUNK + 2 * n + half, w_gate[:, 4 * half:4 * half + 4, n * N:(n + 1) * N], 4)
            for i in range(TILES):
                sp.wait_ge(out_ready, i + 1)
                sp.dma_start(t["y"][0, i * P:(i + 1) * P, :], result[:, i, :]).then_inc(stored, 16)
            sp.wait_ge(stored, 16 * TILES)

        @block.tensor
        def _(pe):
            def mm(out, lhsT, rhs, start, stop):
                return pe.matmul(out, lhsT, rhs, start=start, stop=stop, skip_group_check=True)

            def transpose16(src, done, free=None):
                for j in range(KD // 2):
                    if free:
                        pe.wait_ge(free[0], free[1] + j)
                    for kk in range(2):
                        for i in range(TILES):
                            c = 2 * j + kk
                            last = pe.transpose(ps[:, 4 + j, kk * SEQ + i * P:kk * SEQ + (i + 1) * P],
                                                src[:, i, c * P:(c + 1) * P], ident)
                    last.then_inc(done, 1)

            def project(c0, lhsT, n_bank, first_ready=None, then_ready=None):
                for half in range(2):
                    wait = then_ready if half else first_ready
                    if wait:
                        pe.wait_ge(*wait)
                    chunk_ready(pe, c0 + half)
                    w = ring[:, slot_of(c0 + half), :].rearrange("p (k n) -> p k n", k=4)
                    for i in range(TILES):
                        for kk in range(4):
                            c = 4 * half + kk
                            last = mm(ps[:, n_bank + i, :], lhsT[:, c, i * P:(i + 1) * P], w[:, kk, :],
                                      c == 0, c == KD - 1)
                    last.then_inc(used, 1)

            pe.wait_ge(early_loaded, 16)
            pe.wait_ge(vec_loaded, 16 * 6)
            pe.transpose(ps[:, 0, 0:5 * KD], vec_rows, ident[0:5 * KD, 0:5 * KD])
            pe.wait_ge(pos_cast, 1)
            pe.transpose(ps[:, 0, 64:64 + TILES], pos_row, ident[0:TILES, 0:TILES]).then_inc(vec_psum, 1)

            pe.wait_ge(xn_ready, TILES)
            transpose16(xn, xT_psum)

            def column_block(j):
                if j == 0:
                    pe.wait_ge(vecs_read, 1)
                    pe.wait_ge(hT_ready, 4)
                if j >= 2:
                    pe.wait_ge(*block_read(j - 2))
                project(block_chunk(j), hT, 2 * (j % 2))

            def scores(g):
                if g == 0:
                    pe.wait_ge(qkT_ready, 8)
                    pe.wait_ge(kz_ready, 1)
                    pe.wait_ge(read_act, 2 * 2)
                else:
                    pe.wait_ge(ret_read, g)
                for c in range(TILES):
                    for i in range(4):
                        h = 4 * g + i
                        last = mm(ps[:, 4 + c, i * P:(i + 1) * P], kT[:, h, c * P:(c + 1) * P],
                                  qT[:, h, c * P:(c + 1) * P], True, True)
                    last.then_inc(ret_psum, 1)
                if g:
                    pe.wait_ge(kv_ready, g)
                for i in range(4):
                    h = 4 * g + i
                    last = mm(ps[:, 6, i * P:(i + 1) * P], k[:, 0, h * P:(h + 1) * P],
                              v[:, 0, h * P:(h + 1) * P], True, True)
                last.then_inc(ret_psum, 1)

            def inner(g):
                pe.wait_ge(scores_ready, 2 * g + 2)
                for c in range(TILES):
                    for i in range(4):
                        h = 4 * g + i
                        last = mm(ps[:, 4 + c, i * P:(i + 1) * P], scoresT[:, c, i * P:(i + 1) * P],
                                  v[:, c, h * P:(h + 1) * P], True, True)
                last.then_inc(ret_psum, 1)
                pe.wait_ge(kv_ready, g + 1)
                for i in range(4):
                    h = 4 * g + i
                    last = mm(ps[:, 7, i * P:(i + 1) * P], qT[:, h, P:2 * P], kv[:, i * P:(i + 1) * P], True, True)
                last.then_inc(ret_psum, 1)

            def pool_mix():
                pe.wait_ge(ret_read, 2)
                for j in range(4):
                    for kk in range(2):
                        c = 2 * j + kk
                        m = POOLM + 3 * P * (c // 2)
                        out = ps[:, 4 + j, kk * SEQ:(kk + 1) * SEQ]
                        uc = [u[:, i, c * P:(c + 1) * P] for i in range(TILES)]
                        mm(out[:, 0:P], uc[0], const[:, m:m + P], True, True)
                        mm(out[:, P:2 * P], uc[0], const[:, m + P:m + 2 * P], True, False)
                        last = mm(out[:, P:2 * P], uc[1], const[:, m + 2 * P:m + 3 * P], False, True)
                    last.then_inc(pool_psum, 1)

            def pool_project():
                pe.wait_ge(mixT_ready, 4)
                chunk_ready(pe, POOL_CHUNK)
                w = ring[:, slot_of(POOL_CHUNK), :].rearrange("p (k n) -> p k n", k=8)
                for m in range(KD):
                    for kk in range(2):
                        last = mm(ps[:, 4 + m // 2, (m % 2) * SEQ:(m % 2 + 1) * SEQ],
                                  w[:, 2 * (m // 2) + kk, (m % 2) * P:(m % 2 + 1) * P],
                                  mixedT[:, 2 * (m // 2) + kk, :], kk == 0, kk == 1)
                last.then_inc(used, 1)

            for j in range(4):
                column_block(j)
            pe.wait_ge(const_loaded, 16)
            column_block(4)
            pe.wait_ge(rotated, 4)
            transpose16(q, qkT_psum)
            column_block(5)
            pe.wait_ge(rotated, 8)
            transpose16(k, qkT_psum, free=(qkT_ready, 1))
            column_block(6)
            scores(0)
            column_block(7)
            inner(0)
            column_block(8)
            scores(1)
            column_block(9)
            inner(1)
            column_block(10)
            pool_mix()
            column_block(11)
            pool_project()
            column_block(12)
            column_block(13)
            pe.wait_ge(yret_ready, 1)
            transpose16(ret, yrT_psum, free=(ypT_ready, 1))

            for unit in range(4):
                if unit < 2:
                    pe.wait_ge(*block_read(12 + unit))
                else:
                    pe.wait_ge(branch_read, unit - 1)
                pe.wait_ge(yrT_ready, 4) if unit == 1 else None
                project(BRANCH_CHUNK + 2 * unit, yretT if unit % 2 else ypoolT, 2 * (unit % 2))
                if unit == 2 or unit == 3:
                    pe.wait_ge(branch_read, 2 * unit - 2)
                    for j in (2 * unit - 4, 2 * unit - 3):
                        for kk in range(2):
                            for i in range(TILES):
                                c = 2 * j + kk
                                last = pe.transpose(ps[:, 4 + j, kk * SEQ + i * P:kk * SEQ + (i + 1) * P],
                                                    merged[:, i, c * P:(c + 1) * P], ident)
                        last.then_inc(mT_psum, 1)
            project(OUT_CHUNK, mergedT, 0, (mT_ready, 2), (mT_ready, 4))
            project(OUT_CHUNK + 2, mergedT, 2)

            pe.wait_ge(xn_ready, 2 * TILES)
            transpose16(xn, xT_psum)
            pe.wait_ge(hT_ready, 8)
            pe.wait_ge(router_loaded, 32)
            for i in range(TILES):
                out = ps[:, 0, i * N_EXPERTS:(i + 1) * N_EXPERTS]
                for c in range(KD):
                    mm(out, hT[:, c, i * P:(i + 1) * P], w_router[:, c, :], c == 0, False)
                last = mm(out, ones[0:1, :], b_router, False, True)
            last.then_inc(logits_psum, 1)
            pe.wait_ge(mask_ready, 1)
            out = ps[:, 1, 0:N_EXPERTS]
            mm(out, tri, mask[:, 0, :], True, True)
            out = ps[:, 1, N_EXPERTS:2 * N_EXPERTS]
            mm(out, ones, mask[:, 0, :], True, False)
            mm(out, tri, mask[:, 1, :], False, True)
            out = ps[0:1, 1, 2 * N_EXPERTS:3 * N_EXPERTS]
            mm(out, ones[:, 0:1], mask[:, 0, :], True, False)
            mm(out, ones[:, 0:1], mask[:, 1, :], False, True).then_inc(route_psum, 1)
            pe.wait_ge(comb_ready, 1)
            for i in range(TILES):
                last = pe.transpose(ps[0:N_EXPERTS, 2, i * P:(i + 1) * P], comb[:, i, 0:N_EXPERTS], ident)
            last.then_inc(route_psum, 1)

            def gather(s, pair):
                pe.wait_ge(s.onehot_ready, pair + 1)
                for c in range(KD):
                    for i in range(TILES):
                        last = mm(ps[:, 6 + c // 4, (c % 4) * P:(c % 4 + 1) * P], xn[:, i, c * P:(c + 1) * P],
                                  onehot[:, i, :], i == 0, i == TILES - 1)
                last.then_inc(s.gathered, 1)

            def both(s, pair, i, lhsT, c, columns, bank, start, stop):
                for n in range(len(columns)):
                    for h in range(2):
                        w = ring[:, slot_of(s.base + 2 * i + h), columns[n]:columns[n] + N]
                        last = mm(ps[h * BLOCK:(h + 1) * BLOCK, bank + n, :], lhsT[:, c, h * BLOCK:(h + 1) * BLOCK],
                                  w, start, stop)
                        if stop_chunk(columns[n]) and n == len(columns) - 1:
                            last.then_inc(s.chunk_used, 1)

            def stop_chunk(column):
                return column == SLOT - N

            def gate_up(s, pair):
                pe.wait_ge(s.hg_ready, pair + 1)
                for i in range(UP_CHUNKS):
                    for h in range(2):
                        expert_ready(pe, s, pair, h, i)
                    both(s, pair, i, hg, i, [n * N for n in range(4)], 0, i == 0, False)
                pe.wait_ge(s.bias_loaded, 32 * pair + 32)
                for n in range(4):
                    last = mm(ps[:, n, :], const[0:2, SEL:SEL + P], bias_rows[:, n * N:(n + 1) * N], False, True)
                last.then_inc(s.up_done, 1)

            def act_to_width(s, pair):
                pe.wait_ge(s.act_ready, pair + 1)
                for c in range(KD):
                    last = pe.transpose(ps[:, c // 4, (c % 4) * P:(c % 4 + 1) * P], gate[:, c * P:(c + 1) * P], ident)
                last.then_inc(s.act_xposed, 1)

            def down(s, pair):
                pe.wait_ge(s.actT_ready, pair + 1)
                for i in range(DOWN_CHUNKS):
                    for h in range(2):
                        expert_ready(pe, s, pair, h, UP_CHUNKS + i)
                    for kk in range(2):
                        c = 2 * i + kk
                        both(s, pair, UP_CHUNKS + i, actT, c, [kk * D, kk * D + N], 4, c == 0, c == KD - 1)

            def scatter_weights(s, pair):
                pe.wait_ge(s.sw_ready, pair + 1)
                pe.wait_ge(s.up_read, pair + 1)
                for i in range(TILES):
                    last = pe.transpose(ps[:, 2, i * P:(i + 1) * P], weighted[:, i, :], ident)
                last.then_inc(s.swt_done, 1)

            def scatter(s, pair):
                pe.wait_ge(s.st_ready, pair + 1)
                pe.wait_ge(s.os_ready, pair + 1)
                for i in range(4):
                    tile, n = i // 2, i % 2
                    mm(ps[:, SUM_BANKS[i], :], scatterT[:, tile * P:(tile + 1) * P],
                       slot_rows[:, n * N:(n + 1) * N], True, True).then_inc(s.scattered, 1)

            def project_ple():
                pe.wait_ge(p_loaded, 16)
                pe.wait_ge(proj_loaded, 16)
                for c in range(2):
                    for i in range(TILES):
                        last = pe.transpose(ps[:, 4, c * SEQ + i * P:c * SEQ + (i + 1) * P],
                                            p_in[:, i, c * P:(c + 1) * P], ident)
                last.then_inc(pT_psum, 1)
                pe.wait_ge(pT_ready, 1)
                for i in range(4):
                    tile, n = i // 2, i % 2
                    for c in range(2):
                        last = mm(ps[:, SUM_BANKS[i], :], pT[:, c, tile * P:(tile + 1) * P],
                                  w_proj[:, c, n * N:(n + 1) * N], c == 0, c == 1)
                    last.then_inc(ple_psum, 1)

            def pair_steps(pair, is_first=False):
                if not is_first:
                    pe.wait_ge(first.st_ready, pair)
                gate_up(first, pair)
                if is_first:
                    project_ple()
                else:
                    scatter(first, pair - 1)
                pe.wait_ge(first.acc_done, 4 * pair + 2)
                gather(first, pair + 1)
                scatter_weights(first, pair)
                act_to_width(first, pair)
                pe.wait_ge(first.acc_done, 4 * pair + 4)
                down(first, pair)

            pe.wait_ge(route_ready, 1)
            gather(first, 0)
            for i in range(4):
                tile, n = i // 2, i % 2
                mm(ps[:, (0, 1, 4, 5)[i], :], combT[:, tile * P:(tile + 1) * P], b_down[:, n * N:(n + 1) * N],
                   True, True).then_inc(bias_psum, 1)
            pe.wait_ge(bias_read, 4)
            pair_steps(0, True)
            with pe.Fori(1, PAIRS) as pair:
                pair_steps(pair)
            scatter(first, PAIRS - 1)

            def body(j, e, low):
                pe.wait_ge(first.acc_done, first.acc0 + 4 * PAIRS)
                gather(more, j)
                gate_up(more, j)
                scatter_weights(more, j)
                act_to_width(more, j)
                down(more, j)
                scatter(more, j)
                pe.wait_ge(more.pair_done, j + 1)

            def skipped():
                for s, n in ((more.gathered, 1), (more.chunk_used, PER_PAIR), (more.up_done, 1), (more.swt_done, 1),
                             (more.act_xposed, 1), (more.scattered, 4)):
                    pe.sem_inc(s, n)

            more_pairs("pe", pe, body, skipped)

            pe.wait_ge(xn_ready, 3 * TILES)
            transpose16(xn, xT_psum)
            pe.wait_ge(hT_ready, 12)
            project(PLE_CHUNK, hT, 0)
            project(PLE_CHUNK + 2, hT, 2)

        @block.gpsimd
        def _(pool):
            nc.gpsimd.memset(exponent, -0.5).then_inc(mean_square, 1)
            for turn in range(5):
                if turn == 1:
                    pool.wait_ge(var_ready, 1)
                    src, dst, n, eps = var, var, P, GN_EPS
                else:
                    pool.wait_ge(ss_ready, TILES * (turn + (turn == 0)))
                    src, dst, n, eps = ss, rstd, D, RMS_EPS
                nc.gpsimd.tensor_scalar(dst, src, 1.0 / n, eps, ALU.mult, ALU.add).then_inc(mean_square, 1)
                pool.wait_ge(mean_square, turn + 2)
                nc.gpsimd.tensor_tensor(dst, dst, exponent[:, 0:dst.shape[1]], ALU.pow).then_inc(rstd_ready, 1)

        @block.scalar
        def _(act_eng):
            e = act_eng
            e.dma_start(const[:, 0:EARLY], t["const"][:, 0:EARLY]).then_inc(early_loaded, 16)
            e.dma_start(x[:, :, :], t["x"][0].rearrange("(i p) n -> p i n", p=P)).then_inc(x_loaded, 16)
            for i, g in enumerate((t["g_mix_norm"], t["g_ret_norm"], t["pool_scale"], t["g_ffn_norm"], t["g_ple_norm"])):
                e.dma_start(vec_rows[KD * i:KD * (i + 1), :], g[0].rearrange("(k p) -> k p", p=P)).then_inc(vec_loaded, 16)
            e.dma_start(pos_int, t["positions"][0].rearrange("(i p) -> i p", p=P)).then_inc(vec_loaded, 16)
            e.dma_start(const[:, EARLY:], t["const"][:, EARLY:]).then_inc(const_loaded, 16)

            e.wait_ge(x_loaded, 16)
            for i in range(TILES):
                if i:
                    e.wait_ge(ss_ready, i)
                nc.scalar.activation(waste, x[:, i, :], ACT.Square, accum_out=ss[:, i:i + 1]).then_inc(ss_ready, 1)
            e.wait_ge(angles_ready, 1)
            nc.scalar.activation(sin, angle, ACT.Sin).then_inc(sin_ready, 1)
            nc.scalar.activation(cos, turns, ACT.Sin).then_inc(sin_ready, 1)

            def copies_qk(n):
                for j in range(4):
                    e.wait_ge(qkT_psum, 4 * n + j + 1)
                    nc.scalar.copy((qT, kT)[n][:, 2 * j:2 * j + 2, :], bank_cols(4 + j, 2)).then_inc(qkT_ready, 1)

            def read_block(j, dst, func):
                n = j % 2
                e.wait_ge(used, block_chunk(j) + 2)
                for i in range(TILES):
                    nc.scalar.activation(dst[:, i, n * N:(n + 1) * N], ps[:, 2 * n + i, :], func).then_inc(read_act, 1)

            def read_kv(g):
                e.wait_ge(ret_psum, 5 * g + 3)
                nc.scalar.copy(kv, ps[:, 6, :]).then_inc(kv_ready, 1)

            read_block(4, v, ACT.Copy)
            copies_qk(0)
            read_block(5, v, ACT.Copy)
            copies_qk(1)
            e.wait_ge(rotated, 8)
            read_block(6, u, ACT.Copy)
            read_kv(0)
            read_block(7, u, ACT.Copy)

            def silu_block(j):
                n = j % 2
                e.wait_ge(used, block_chunk(j) + 2)
                for i in range(TILES):
                    nc.scalar.activation(silu_g[:, i, n * N:(n + 1) * N], ps[:, 2 * n + i, :], ACT.Sigmoid).then_inc(sig_g, 1)

            silu_block(8)
            e.wait_ge(ret_read, 1)
            read_kv(1)
            silu_block(9)
            e.wait_ge(ret_read, 2)
            read_block(10, gates[0], ACT.Sigmoid)
            for j in range(4):
                e.wait_ge(pool_psum, j + 1)
                nc.scalar.copy(mixedT[:, 2 * j:2 * j + 2, :], bank_cols(4 + j, 2)).then_inc(mixT_ready, 1)
            e.dma_start(b_down, t["b_down"][0]).then_inc(late_loaded, 16)
            e.dma_start(g_final, t["g_final"].unsqueeze(0).to_broadcast([P, D])).then_inc(late_loaded, 16)
            e.wait_ge(square_in, 1)
            nc.scalar.activation(square, ret, ACT.Square).then_inc(squared, 1)
            read_block(11, gates[0], ACT.Sigmoid)
            read_block(12, gates[1], ACT.Sigmoid)
            read_block(13, gates[1], ACT.Sigmoid)
            for j in range(4):
                e.wait_ge(mT_psum, j + 1)
                nc.scalar.copy(mergedT[:, 2 * j:2 * j + 2, :], bank_cols(4 + j, 2)).then_inc(mT_ready, 1)
            e.wait_ge(branch_read, 4)
            e.dma_start(w_router, t["w_router"][0].rearrange("(k p) n -> p k n", p=P)).then_inc(router_loaded, 16)
            e.dma_start(b_router, t["b_router"]).then_inc(router_loaded, 16)
            e.dma_start(w_proj, t["w_ple_proj"][0].rearrange("(c p) n -> p c n", p=P)).then_inc(proj_loaded, 16)
            e.dma_start(p_in, t["p"][0, 0].rearrange("(i p) n -> p i n", p=P)).then_inc(p_loaded, 16)

            for i in range(TILES):
                e.wait_ge(x_ready, i + 1)
                nc.scalar.activation(xn[:, i, :], x[:, i, :], ACT.Square,
                                     accum_out=ss[:, i:i + 1]).then_inc(ss_ready, 1)
            e.wait_ge(exp_in, 1)
            for i in range(TILES):
                nc.scalar.activation(expo[:, i, :], logit[:, i, 0:N_EXPERTS], ACT.Exp,
                                     bias=neg[:, i:i + 1]).then_inc(exp_ready, 1)

            def load_bias(s, experts):
                for h, ex in enumerate(experts):
                    e.dma_start(bias_rows[h:h + 1, :], t["b_gate_up"][0, bass.ds(ex, 1), :]).then_inc(s.bias_loaded, 16)

            def sigmoid(s, pair):
                e.wait_ge(s.gate_ready, pair + 1)
                nc.scalar.activation(sig, gate, ACT.Sigmoid, scale=ALPHA).then_inc(s.sig_ready, 1)

            def read_actT(s, pair):
                e.wait_ge(s.act_xposed, pair + 1)
                nc.scalar.copy(B[2][:, 0:D], two_banks(0)).then_inc(s.actT_ready, 1)

            def read_down(s, pair):
                e.wait_ge(s.chunk_used, s.base + PER_PAIR * pair + PER_PAIR)
                nc.scalar.copy(slot_rows, two_banks(4)).then_inc(s.os_ready, 1)

            e.wait_ge(used, EXPERT_CHUNK)
            load_bias(first, (0, 1))
            e.wait_ge(pT_psum, 1)
            nc.scalar.copy(pT, bank_cols(4, 2)).then_inc(pT_ready, 1)
            sigmoid(first, 0)
            read_actT(first, 0)
            read_down(first, 0)
            with e.Fori(1, PAIRS) as pair:
                load_bias(first, (2 * pair, 2 * pair + 1))
                sigmoid(first, pair)
                read_actT(first, pair)
                read_down(first, pair)

            def body(j, ex, low):
                e.wait_ge(first.scattered, 4 * PAIRS)
                load_bias(more, (ex, ex))
                sigmoid(more, j)
                read_actT(more, j)
                read_down(more, j)
                e.wait_ge(more.pair_done, j + 1)

            def skipped():
                for s, n in ((more.bias_loaded, 32), (more.sig_ready, 1), (more.actT_ready, 1), (more.os_ready, 1)):
                    e.sem_inc(s, n)

            more_pairs("act", e, body, skipped)
            e.wait_ge(x_ready, 2 * TILES)
            for i in range(TILES):
                nc.scalar.activation(xn[:, i, :], x[:, i, :], ACT.Square,
                                     accum_out=ss[:, i:i + 1]).then_inc(ss_ready, 1)
            for n in range(2):
                e.wait_ge(used, PLE_CHUNK + 2 * n + 2)
                if n:
                    e.wait_ge(x_ready, 3 * TILES)
                for i in range(TILES):
                    nc.scalar.activation(ple_gate[:, i, :], ps[:, 2 * n + i, :], ACT.Sigmoid).then_inc(gate_sig, 1)
            for i in range(TILES):
                e.wait_ge(x_ready, 3 * TILES + i + 1)
                nc.scalar.activation(xn[:, i, :], x[:, i, :], ACT.Square,
                                     accum_out=ss[:, i:i + 1]).then_inc(ss_ready, 1)

        @block.vector
        def _(dve):
            ve = nc.vector
            counts_of = {}

            order = [vec_order]

            def step(ins, s=None):
                s = s or order[0]
                c = counts_of.setdefault(id(s), Count())
                ins.then_inc(s, 1)
                c.n += 1
                dve.wait_ge(s, c.value())

            def own(s):
                return counts_of.setdefault(id(s), Count())

            dve.wait_ge(vec_loaded, 16 * 6)
            step(ve.tensor_copy(pos_row, pos_int), pos_cast)
            dve.wait_ge(vec_psum, 1)
            step(ve.tensor_copy(vecs[:, :], ps[:, 0, 0:5 * KD]))
            step(ve.tensor_copy(pos, ps[:, 0, 64:64 + TILES]), vecs_read)

            def normalise(n):
                dve.wait_ge(rstd_ready, (1, 3, 4)[n])
                for i in range(TILES):
                    step(ve.tensor_scalar(xn[:, i, :], x[:, i, :], rstd[:, i:i + 1], None, ALU.mult), xn_ready)
                g = (G_MIX, G_FFN, G_PLE)[n]
                for j in range(4):
                    dve.wait_ge(xT_psum, 4 * n + j + 1)
                    step(ve.tensor_tensor(hT[:, 2 * j:2 * j + 2, :], bank_cols(4 + j, 2),
                                          across(vecs[:, g + 2 * j:g + 2 * j + 2], SEQ), ALU.mult), hT_ready)

            normalise(0)
            for i in range(TILES):
                step(ve.tensor_scalar(cos[:, i, :], const[:, INVF:INVF + 64], pos[:, i:i + 1], None, ALU.mult))
            for dst, shift in ((angle, 0.0), (turns, 0.25)):
                step(ve.tensor_scalar(nsin, cos, 1.0 / 6.283185307179586, shift, ALU.mult, ALU.add))
                step(ve.tensor_scalar(nsin, nsin, ROUND, None, ALU.add))
                step(ve.tensor_scalar(nsin, nsin, ROUND, None, ALU.subtract))
                step(ve.scalar_tensor_tensor(dst, nsin, -TWO_PI_HI, cos, ALU.mult, ALU.add))
                step(ve.scalar_tensor_tensor(dst, nsin, -TWO_PI_MID, dst, ALU.mult, ALU.add))
                step(ve.scalar_tensor_tensor(dst, nsin, -TWO_PI_LO, dst, ALU.mult, ALU.add))
                if shift:
                    step(ve.tensor_scalar(dst, dst, 1.5707963267948966, None, ALU.add))
                last = ve.tensor_scalar(dst, dst, 3.1415925, -3.1415925, ALU.min, ALU.max)
                step(last, angles_ready if shift else None)
            dve.wait_ge(sin_ready, 2)
            step(ve.tensor_scalar(nsin, sin, -1.0, None, ALU.mult))

            def heads4(ap):
                return ap.rearrange("p (h x f) -> p h x f", h=4, x=2)

            def per_head(ap, n):
                return ap.unsqueeze(1).to_broadcast([P, n, 64])

            for j in range(4):
                n, dst = j % 2, (q if j < 2 else k)
                dve.wait_ge(used, block_chunk(j) + 2)
                for i in range(TILES):
                    src = heads4(ps[:, 2 * n + i, :])
                    step(ve.tensor_tensor(rot_a.rearrange("p (h f) -> p h f", f=64),
                                          ps[:, 2 * n + i, :].rearrange("p (h f) -> p h f", f=64),
                                          per_head(cos[:, i, :], 8), ALU.mult))
                    step(ve.tensor_tensor(heads4(rot_b)[:, :, 0, :], src[:, :, 1, :], per_head(nsin[:, i, :], 4), ALU.mult))
                    step(ve.tensor_tensor(heads4(rot_b)[:, :, 1, :], src[:, :, 0, :], per_head(sin[:, i, :], 4), ALU.mult), read_dve)
                    step(ve.tensor_tensor(dst[:, i, n * N:(n + 1) * N], rot_a, rot_b, ALU.add), rotated)
            dve.wait_ge(const_loaded, 16)
            dve.wait_ge(qkT_psum, 8)
            k0 = k[:, 0, :].rearrange("p (h f) -> p h f", f=P)
            step(ve.tensor_tensor(k0, k0, across(const[:, ZETA:ZETA + HEADS], P), ALU.mult), kz_ready)

            def decay_scores(g):
                for c in range(TILES):
                    dve.wait_ge(ret_psum, 5 * g + c + 1)
                    step(ve.tensor_tensor(scoresT[:, c, 0:N], ps[:, 4 + c, :],
                                          const[:, DMAT + g * N:DMAT + (g + 1) * N], ALU.mult), scores_ready)

            def read_ret(g):
                dve.wait_ge(ret_psum, 5 * g + 4)
                step(ve.tensor_copy(ret[:, 0, g * N:(g + 1) * N], ps[:, 4, :]))
                dve.wait_ge(ret_psum, 5 * g + 5)
                step(ve.tensor_tensor(cross.rearrange("p (h f) -> p h f", f=P), bank_cols(7, 4),
                                      across(const[:, XI + 4 * g:XI + 4 * g + 4], P), ALU.mult))
                step(ve.tensor_tensor(ret[:, 1, g * N:(g + 1) * N], cross, ps[:, 5, :], ALU.add), ret_read)

            def silu(j):
                n = j % 2
                for i in range(TILES):
                    dve.wait_ge(sig_g, 2 * (j - 8) + i + 1)
                    z = silu_g[:, i, n * N:(n + 1) * N]
                    step(ve.tensor_tensor(z, z, ps[:, 2 * n + i, :], ALU.mult), read_dve)

            decay_scores(0)
            read_ret(0)
            silu(8)
            decay_scores(1)
            silu(9)
            read_ret(1)
            flat = [z.rearrange("p t (h f) -> p (t h) f", f=P) for z in (ret, square)]
            step(ve.tensor_reduce(mean, flat[0], AX.X, ALU.add))
            step(ve.tensor_scalar(mean, mean, 1.0 / P, None, ALU.mult))
            step(ve.tensor_tensor(flat[0], flat[0], across(mean, P), ALU.subtract), square_in)
            dve.wait_ge(squared, 1)
            step(ve.tensor_reduce(var, flat[1], AX.X, ALU.add), var_ready)
            dve.wait_ge(rstd_ready, 2)
            step(ve.tensor_tensor(flat[0], flat[0], across(var, P), ALU.mult))
            step(ve.tensor_tensor(ret, ret, silu_g, ALU.mult), yret_ready)
            dve.wait_ge(used, POOL_CHUNK + 1)
            for j in range(4):
                step(ve.tensor_tensor(ypoolT[:, 2 * j:2 * j + 2, :], bank_cols(4 + j, 2),
                                      across(vecs[:, G_POOL + 2 * j:G_POOL + 2 * j + 2], SEQ), ALU.mult), ypT_ready)
            for j in range(4):
                dve.wait_ge(yrT_psum, j + 1)
                step(ve.tensor_tensor(yretT[:, 2 * j:2 * j + 2, :], bank_cols(4 + j, 2),
                                      across(vecs[:, G_RET + 2 * j:G_RET + 2 * j + 2], SEQ), ALU.mult), yrT_ready)
            dve.wait_ge(read_act, 2 * 8)
            for unit in range(4):
                n, is_a = unit // 2, unit % 2
                dve.wait_ge(used, BRANCH_CHUNK + 2 * unit + 2)
                for i in range(TILES):
                    m = merged[:, i, n * N:(n + 1) * N]
                    g = gates[1 - is_a][:, i, n * N:(n + 1) * N]
                    final = branch_read if i == TILES - 1 else None
                    if is_a:
                        step(ve.tensor_tensor(branch_tmp, g, ps[:, 2 + i, :], ALU.mult))
                        step(ve.tensor_tensor(m, m, branch_tmp, ALU.add), final)
                    else:
                        step(ve.tensor_tensor(m, g, ps[:, i, :], ALU.mult), final)
            for n in range(2):
                dve.wait_ge(used, OUT_CHUNK + 2 * n + 2)
                for i in range(TILES):
                    z = x[:, i, n * N:(n + 1) * N]
                    step(ve.tensor_tensor(z, z, ps[:, 2 * n + i, :], ALU.add), x_ready if n else None)
            normalise(1)
            dve.wait_ge(logits_psum, 1)
            step(ve.memset(logit[:, :, N_EXPERTS:], BIG))
            step(ve.tensor_copy(logit[:, :, 0:N_EXPERTS], ps[:, 0, 0:TILES * N_EXPERTS].rearrange("p (t e) -> p t e", t=TILES)))
            for i in range(TILES):
                step(ve.max(top[:, i, :], logit[:, i, 0:N_EXPERTS]))
            step(ve.tensor_scalar(neg.unsqueeze(2), top[:, :, 0:1], -1.0, None, ALU.mult), exp_in)
            step(ve.memset(top[:, :, TOP_K:8], BIG))
            for i in range(TILES):
                step(ve.match_replace(marked[:, i, :], top[:, i, :], logit[:, i, :], -BIG))
            step(ve.tensor_scalar(mask, marked[:, :, 0:N_EXPERTS], -BIG, None, ALU.is_equal), mask_ready)
            dve.wait_ge(exp_ready, TILES)
            step(ve.memset(comb[:, :, N_EXPERTS:], 0.0))
            step(ve.memset(rank[:, :, N_EXPERTS:], -1.0))
            step(ve.tensor_tensor(expo, expo, mask, ALU.mult))
            step(ve.tensor_reduce(tot, expo, AX.X, ALU.add))
            step(ve.reciprocal(tot, tot))
            step(ve.tensor_tensor(comb[:, :, 0:N_EXPERTS], expo, across(tot, N_EXPERTS), ALU.mult), comb_ready)
            dve.wait_ge(route_psum, 1)
            r = rank[:, :, 0:N_EXPERTS]
            step(ve.scalar_tensor_tensor(r, ps[:, 1, 0:TILES * N_EXPERTS].rearrange("p (t e) -> p t e", t=TILES), 1.0,
                                         mask, ALU.add, ALU.mult))
            step(ve.tensor_scalar(r, r, 1.0, None, ALU.subtract))
            step(ve.tensor_copy(count_f, ps[0:1, 1, 2 * N_EXPERTS:3 * N_EXPERTS]))
            step(ve.tensor_copy(counts, count_f))
            step(ve.tensor_reduce(count_top_f, count_f, AX.X, ALU.max))
            step(ve.tensor_copy(count_top, count_top_f))
            dve.wait_ge(route_psum, 2)
            dve.wait_ge(late_loaded, 32)
            step(ve.tensor_copy(combT, ps[0:N_EXPERTS, 2, 0:SEQ]), route_ready)

            def make_onehot(s, experts, lows=(0, 0)):
                for h, (e, low) in enumerate(zip(experts, lows)):
                    for i in range(TILES):
                        last = h == 1 and i == TILES - 1
                        step(ve.tensor_scalar(onehot[:, i, h * BLOCK:(h + 1) * BLOCK],
                                              const[:, IOTA + low:IOTA + low + BLOCK],
                                              rank[:, i, bass.ds(e, 1)], None, ALU.is_equal),
                             s.onehot_ready if last else None)

            def make_weighted(s, experts, lows=(0, 0)):
                for h, (e, low) in enumerate(zip(experts, lows)):
                    for i in range(TILES):
                        last = h == 1 and i == TILES - 1
                        step(ve.tensor_scalar(weighted[:, i, h * BLOCK:(h + 1) * BLOCK],
                                              const[:, IOTA + low:IOTA + low + BLOCK],
                                              rank[:, i, bass.ds(e, 1)], comb[:, i, bass.ds(e, 1)],
                                              ALU.is_equal, ALU.mult), s.sw_ready if last else None)

            def read_gather(s, pair):
                dve.wait_ge(s.gathered, pair + 1)
                src = two_banks(6).rearrange("p (k s) -> p k s", k=KD)
                step(ve.tensor_tensor(hg, src, across(vecs[:, G_FFN:G_FFN + KD], P), ALU.mult), s.hg_ready)

            def clamp(s, pair):
                dve.wait_ge(s.up_done, pair + 1)
                step(ve.tensor_scalar(gate, two_banks(0), LIMIT, None, ALU.min), s.gate_ready)
                step(ve.tensor_scalar(up, two_banks(2), LIMIT, -LIMIT, ALU.min, ALU.max), s.up_read)

            def activate(s, pair):
                step(ve.scalar_tensor_tensor(up, up, 1.0, gate, ALU.add, ALU.mult))
                dve.wait_ge(s.sig_ready, pair + 1)
                step(ve.tensor_tensor(gate, up, sig, ALU.mult), s.act_ready)

            def read_weights(s, pair):
                dve.wait_ge(s.swt_done, pair + 1)
                step(ve.tensor_copy(scatterT, ps[:, 2, 0:SEQ]), s.st_ready)

            def accumulate(s, pair):
                for i in range(4):
                    dve.wait_ge(s.scattered, 4 * pair + i + 1)
                    tile, n = i // 2, i % 2
                    z = x[:, tile, n * N:(n + 1) * N]
                    step(ve.tensor_tensor(z, z, ps[:, SUM_BANKS[i], :], ALU.add), s.acc_done)

            def pair_steps(pair, is_first=False):
                make_onehot(first, (2 * pair + 2, 2 * pair + 3))
                make_weighted(first, (2 * pair, 2 * pair + 1))
                clamp(first, pair)
                if is_first:
                    for i in range(4):
                        dve.wait_ge(ple_psum, i + 1)
                        tile, n = i // 2, i % 2
                        step(ve.tensor_copy(ple[:, tile, n * N:(n + 1) * N], ps[:, SUM_BANKS[i], :]), first.acc_done)
                else:
                    accumulate(first, pair - 1)
                activate(first, pair)
                read_gather(first, pair + 1)
                read_weights(first, pair)

            make_onehot(first, (0, 1))
            read_gather(first, 0)
            for i in range(4):
                dve.wait_ge(bias_psum, i + 1)
                tile, n = i // 2, i % 2
                z = x[:, tile, n * N:(n + 1) * N]
                step(ve.tensor_tensor(z, z, ps[:, (0, 1, 4, 5)[i], :], ALU.add), bias_read)
            pair_steps(0, True)

            def per_turn(s, order_sem):
                return {s.onehot_ready: 1, s.sw_ready: 1, s.gate_ready: 1, s.up_read: 1, s.acc_done: 4,
                        s.act_ready: 1, s.hg_ready: 1, s.st_ready: 1, order_sem: 3 + 3 + 1}

            turn = per_turn(first, vec_order)
            with dve.Fori(1, PAIRS) as pair:
                for s, n in turn.items():
                    own(s).enter(pair - 1, n)
                pair_steps(pair)
                for s in turn:
                    own(s).leave(PAIRS - 1)
            accumulate(first, PAIRS - 1)

            more_turn = per_turn(more, more.order)

            def body(j, e, low):
                for s, n in more_turn.items():
                    own(s).n, own(s).base = 0, j * n
                make_onehot(more, (e, e), (low, low + BLOCK))
                make_weighted(more, (e, e), (low, low + BLOCK))
                read_gather(more, j)
                clamp(more, j)
                activate(more, j)
                read_weights(more, j)
                accumulate(more, j)
                dve.sem_inc(more.pair_done, 1)
                for s, n in more_turn.items():
                    assert own(s).n == n, (s, own(s).n, n)

            def skipped():
                for s, n in more_turn.items():
                    dve.sem_inc(s, n)
                dve.sem_inc(more.pair_done, 1)

            order[0] = more.order
            more_pairs("dve", dve, body, skipped)
            order[0] = vec_order

            dve.sem_inc(x_ready, TILES)
            own(x_ready).n += TILES
            normalise(2)
            for n in range(2):
                for i in range(TILES):
                    dve.wait_ge(gate_sig, 2 * n + i + 1)
                    z = x[:, i, n * N:(n + 1) * N]
                    g = ple_gate[:, i, :]
                    step(ve.tensor_tensor(g, g, ple[:, i, n * N:(n + 1) * N], ALU.mult))
                    step(ve.tensor_tensor(z, z, g, ALU.add), x_ready)
            dve.wait_ge(rstd_ready, 5)
            for i in range(TILES):
                step(ve.scalar_tensor_tensor(result[:, i, :], x[:, i, :], rstd[:, i:i + 1], g_final,
                                             ALU.mult, ALU.mult), out_ready)


def constants():
    import numpy as np
    c = np.zeros((P, N_CONST), np.float32)
    r = np.arange(P)
    c[:, IDENT:IDENT + P] = np.eye(P)
    c[:, INVF:INVF + 64] = np.power(np.float32(10000.0), -(np.arange(64, dtype=np.float32) / np.float32(64)))
    c[:, TRI:TRI + P] = r[:, None] < r[None, :]
    c[:, ONES:ONES + P] = 1.0
    c[:, IOTA:DMAT] = np.arange(DMAT - IOTA)
    scale = float(P) ** -0.5
    log_gamma = np.log1p(-np.exp2(-5.0 - np.arange(HEADS)))
    for h in range(HEADS):
        d = r[None, :] - r[:, None]
        c[:, DMAT + h * P:DMAT + (h + 1) * P] = np.where(d >= 0, np.exp(log_gamma[h] * np.maximum(d, 0)) * scale, 0)
        c[:, ZETA + h] = np.exp(log_gamma[h] * (P - 1 - r)) * scale
        c[:, XI + h] = np.exp(log_gamma[h] * (r + 1))
    for h in range(2):
        c[h, SEL + h * BLOCK:SEL + (h + 1) * BLOCK] = 1.0
    pos = np.arange(SEQ)
    for i, w in enumerate(WINDOWS):
        lag = pos[None, :] - pos[:, None]
        m = ((lag >= 0) & (lag < w)) / np.minimum(pos + 1, w)[None, :] - np.eye(SEQ)
        at = POOLM + 3 * P * i
        c[:, at:at + P], c[:, at + P:at + 2 * P], c[:, at + 2 * P:at + 3 * P] = m[:P, :P], m[:P, P:], m[P:, P:]
    return c


_INS = ["x", "p", "positions", "g_mix_norm", "w_in", "g_ret_norm", "w_pool", "pool_scale", "w_branch", "w_out",
        "g_ffn_norm", "w_router", "b_router", "w_gate_up", "b_gate_up", "w_down", "b_down", "g_ple_norm",
        "w_ple_gate", "w_ple_proj", "g_final"]


def kernel(**inputs):
    import numpy as np
    import concourse.bacc as bacc
    from concourse.bass_utils import run_bass_kernel_spmd

    nc = bacc.Bacc("TRN2", target_bir_lowering=False, num_devices=1)
    arrays = {f"in_{n}": np.ascontiguousarray(inputs[n]) for n in _INS}
    arrays["in_const"] = constants()
    tensors = {n[3:]: nc.dram_tensor(n, a.shape, mybir.dt.from_np(a.dtype), kind="ExternalInput").ap()
               for n, a in arrays.items()}
    tensors["y"] = nc.dram_tensor("out_y", (1, SEQ, D), F32, kind="ExternalOutput").ap()
    build(nc, tensors)
    return run_bass_kernel_spmd(nc, [arrays], core_ids=[0]).results[0]["out_y"]
```

```python
from contextlib import ExitStack

import concourse.bass as bass
from concourse import mybir

F32 = mybir.dt.float32
F32R = mybir.dt.float32r
I32 = mybir.dt.int32
ALU = mybir.AluOpType
ACT = mybir.ActivationFunctionType
AX = mybir.AxisListType

P = 128
SEQ, D = 256, 1024
TILES = SEQ // P
KD = D // P
HEADS = 8
N_EXPERTS, TOP_K = 32, 4
WINDOWS = (2, 4, 8, 16)
BLOCK = 64
BLOCKS_MAX = SEQ // BLOCK
RMS_EPS, GN_EPS = 1e-6, 1e-5
LIMIT, ALPHA = 7.0, 1.702
BIG = 3.0e38
TWO_PI_HI, TWO_PI_MID = 6.28125, 0.0019350051879882812
TWO_PI_LO = 6.283185307179586 - TWO_PI_HI - TWO_PI_MID
ROUND = 12582912.0

SLOTS, SLOT = 12, 2048
N = 512
COLUMN_BLOCKS = [0, 1, 2, 3, 4, 5, 8, 9, 6, 7, 10, 11, 12, 13]
POOL_AFTER = 12
MIXER_SLOTS = 6
POOL_CHUNK = 2 * POOL_AFTER
BRANCH, OUT = len(COLUMN_BLOCKS), len(COLUMN_BLOCKS) + 4
MIXER_BLOCKS = OUT + 2
MIXER_CHUNKS = 2 * MIXER_BLOCKS + 1
PARTS = 4
PIECE = 2 * N
PIECES = 6
UP_CHUNKS, DOWN_CHUNKS = 8, 4
PER_EXPERT = UP_CHUNKS + DOWN_CHUNKS
PER_PAIR = 2 * PER_EXPERT
PAIRS = N_EXPERTS // 2
EXTRAS = 5
REST_PAIR = PAIRS // 2
PLE_CHUNK = PAIRS * PER_PAIR
PLE_BLOCK = MIXER_BLOCKS


def chunk_of(piece):
    c = piece // 2
    return c + (c >= POOL_CHUNK)


def ahead(block):
    return min(PARTS * (block + 1) + PIECES, PARTS * MIXER_BLOCKS)


IDENT, INVF = 0, P
EARLY = INVF + 64
TRI = EARLY
ONES = TRI + P
IOTA = ONES + P
DMAT = IOTA + BLOCKS_MAX * BLOCK + BLOCK
ZETA = DMAT + HEADS * P
XI = ZETA + HEADS
SEL = XI + HEADS
POOLM = SEL + P
N_CONST = POOLM + 3 * len(WINDOWS) * P

G_MIX, G_RET, G_POOL, G_FFN, G_PLE = (KD * i for i in range(5))


class ExpertSemaphores:

    def __init__(self, sem, tag):
        self.onehot_ready = sem(tag + "_onehot_ready")
        self.gathered = sem(tag + "_gathered")
        self.hg_ready = sem(tag + "_hg_ready")
        self.bias_loaded = sem(tag + "_bias_loaded")
        self.gate_ready = sem(tag + "_gate_ready")
        self.up_read = sem(tag + "_up_read")
        self.sig_ready = sem(tag + "_sig_ready")
        self.act_ready = sem(tag + "_act_ready")
        self.act_xposed = sem(tag + "_act_xposed")
        self.actT_ready = sem(tag + "_actT_ready")
        self.os_ready = sem(tag + "_os_ready")
        self.sw_ready = sem(tag + "_sw_ready")
        self.swt_done = sem(tag + "_swt_done")
        self.st_ready = sem(tag + "_st_ready")
        self.scattered = sem(tag + "_scattered")
        self.acc_done = sem(tag + "_acc_done")
        self.chunk_used = sem(tag + "_chunk_used")
        self.pair_done = sem(tag + "_pair_done")
        self.order = sem(tag + "_order")
        self.loaded = [sem(f"{tag}_loaded{i}") for i in range(SLOTS)]


class Count:

    def __init__(self):
        self.n, self.base = 0, 0

    def enter(self, turns_before, per_turn):
        self.start, self.per_turn, self.before = self.n, per_turn, self.n
        self.base, self.n = turns_before * per_turn, self.n

    def leave(self, turns):
        assert self.n - self.before == self.per_turn, (self.n - self.before, self.per_turn)
        self.base, self.n = 0, self.before + turns * self.per_turn

    def value(self):
        return self.base + self.n


def build(nc, t):
    ctx = ExitStack()
    with ctx:
        def sem(name):
            return ctx.enter_context(nc.semaphore(name))

        def sb(name, shape, over=None, before=0):
            views = []
            if over:
                with ExitStack() as freed:
                    if before:
                        freed.enter_context(nc.sbuf_tensor(name + "_before", [P, before], F32))
                    for n, part in over:
                        views.append(freed.enter_context(nc.sbuf_tensor(n, part, F32R)))
            return [ctx.enter_context(nc.sbuf_tensor(name, shape, F32))] + views

        pieces = [P, PIECES, PIECE]
        ring, w_hi, w_lo = sb("ring", [P, SLOTS, SLOT], (("w_hi", pieces), ("w_lo", pieces)), MIXER_SLOTS * SLOT)
        x, = sb("x", [P, TILES, D])
        transposed = [P, KD, SEQ]
        xn, over_xn = sb("xn", [P, TILES, D], (("over_xn", transposed),))
        hT, over_hT = sb("hT", transposed, (("over_hT", transposed),))
        B = [sb(f"B{i}", [P, 2048], ((f"over_B{i}", transposed),)) for i in range(9)]
        over_B2, over_B3, over_B4, over_B5 = (B[i][1] for i in (2, 3, 4, 5))
        B = [buffers[0] for buffers in B]
        const, = sb("const", [P, N_CONST])
        vecs, = sb("vecs", [P, 5 * KD])
        small, = sb("small", [P, 64])

        hT_parts = (over_hT, over_xn)
        ypoolT_parts = (over_B4, over_B2)
        yretT_parts = (over_B3, over_hT)
        mergedT_parts = (over_B5, over_xn)
        ps = ctx.enter_context(nc.psum_tensor("ps", [P, 8, N], F32))

        ident = const[:, IDENT:IDENT + P]
        tri = const[:, TRI:TRI + P]
        ones = const[:, ONES:ONES + P]

        def rows(buf, width=D):
            return buf[:, 0:TILES * width].rearrange("p (t n) -> p t n", t=TILES)

        def cols(buf):
            return buf[:, :].rearrange("p (k s) -> p k s", k=KD)

        q, ret = rows(B[0]), rows(B[0])
        k = rows(B[1])
        scoresT = B[1][:, D:2 * D].rearrange("p (c n) -> p c n", c=TILES)
        square, merged = rows(B[1]), rows(B[1])
        v, mixedT = rows(B[2]), cols(B[2])
        qT, kT = cols(B[3]), cols(B[4])
        rot_a, rot_b = B[4][:, 0:N], B[4][:, N:2 * N]
        silu_g = rows(B[5])
        kv, cross = B[6][:, 0:N], B[6][:, N:2 * N]
        gates = [rows(B[6]), rows(B[7])]
        u = rows(B[8])
        branch_tmp = B[0][:, 0:N]
        vec_rows = B[6][0:5 * KD, 0:P]
        pos_int = B[6][0:TILES, P:2 * P].bitcast(I32)
        pos_row = B[6][0:TILES, 2 * P:3 * P]
        angle = B[7][:, 0:P].rearrange("p (t f) -> p t f", t=TILES)
        turns = B[7][:, P:2 * P].rearrange("p (t f) -> p t f", t=TILES)
        cos = B[8][:, 2 * P:3 * P].rearrange("p (t f) -> p t f", t=TILES)
        sin = B[8][:, 3 * P:4 * P].rearrange("p (t f) -> p t f", t=TILES)
        nsin = B[8][:, 4 * P:5 * P].rearrange("p (t f) -> p t f", t=TILES)
        scratch = B[8][:, D:2 * D]
        hg = B[0][:, 0:D].rearrange("p (k s) -> p k s", k=KD)
        gate, up, sig = B[0][:, D:2 * D], B[1][:, 0:D], B[1][:, D:2 * D]
        bias_rows = B[5][0:2, :]
        bias_rows_first = B[0][0:2, :]
        actT = B[2][:, 0:D].rearrange("p (k s) -> p k s", k=KD)
        slot_rows = B[2][:, D:2 * D]
        scatterT = B[3][:, 0:SEQ]
        onehot, weighted = (B[3][:, i:i + SEQ].rearrange("p (t s) -> p t s", t=TILES) for i in (256, 512))
        p_in = B[3][:, 768:1280].rearrange("p (t n) -> p t n", t=TILES)
        pT = B[3][:, 1280:1792].rearrange("p (c s) -> p c s", c=2)
        EP = N_EXPERTS + 2
        at = [0]

        def piece(n):
            at[0] += n
            return B[4][:, at[0] - n:at[0]]

        combT = piece(SEQ)[0:N_EXPERTS, :]
        rank = piece(TILES * EP).rearrange("p (t e) -> p t e", t=TILES)
        comb = piece(TILES * EP).rearrange("p (t e) -> p t e", t=TILES)
        logit = piece(TILES * 36).rearrange("p (t e) -> p t e", t=TILES)
        marked = piece(TILES * 36).rearrange("p (t e) -> p t e", t=TILES)
        top = piece(TILES * 8).rearrange("p (t e) -> p t e", t=TILES)
        mask = piece(TILES * N_EXPERTS).rearrange("p (t e) -> p t e", t=TILES)
        mask_flat = mask.rearrange("p t e -> p (t e)")
        expo = piece(TILES * N_EXPERTS).rearrange("p (t e) -> p t e", t=TILES)
        counts = piece(N_EXPERTS)[0:1, :].bitcast(I32)
        count_f = piece(N_EXPERTS)[0:1, :]
        count_top = piece(1)[0:1, :].bitcast(I32)
        count_top_f = piece(1)[0:1, :]
        w_router = piece(KD * N_EXPERTS).rearrange("p (k e) -> p k e", k=KD)
        b_router = piece(N_EXPERTS)
        logitT = piece(SEQ)[0:N_EXPERTS, :]
        assert at[0] <= 2048
        w_proj = B[6][:, :].rearrange("p (c n) -> p c n", c=2)
        ple = rows(B[7])
        b_down = B[8][0:N_EXPERTS, 0:D]
        g_final = B[8][:, D:2 * D]
        result = rows(B[0])
        ple_gate = B[1][:, :].rearrange("p (h t n) -> p h t n", h=2, t=TILES)

        pos, ss, rstd, neg, tot = (small[:, 2 * i:2 * i + 2] for i in range(5))
        ss_half = small[:, 10:10 + 2 * TILES].rearrange("p (n t) -> p n t", n=2)
        mean, var, exponent = (small[:, i:i + 16] for i in (16, 32, 48))

        x_loaded = [sem(f"x_loaded{i}") for i in range(TILES)]
        vec_loaded, early_loaded, const_loaded = map(sem, ("vec_loaded", "early_loaded", "const_loaded"))
        router_loaded, late_loaded = sem("router_loaded"), sem("late_loaded")
        p_loaded, proj_loaded, stored = map(sem, ("p_loaded", "proj_loaded", "stored"))
        vec_order = sem("vec_order")
        extra_loaded = [sem(f"extra_loaded{i}") for i in range(EXTRAS)]
        mixer_loaded = [sem(f"mixer_loaded{i}") for i in range(MIXER_SLOTS)]
        hi_ready, lo_ready = sem("hi_ready"), sem("lo_ready")
        piece_used = sem("piece_used")
        hT_hi, ypT_hi, yrT_hi, mT_hi = map(sem, ("hT_hi", "ypT_hi", "yrT_hi", "mT_hi"))
        pool_projected = sem("pool_projected")
        pos_cast, vec_psum, vecs_read = map(sem, ("pos_cast", "vec_psum", "vecs_read"))
        angles_ready, sin_ready = sem("angles_ready"), sem("sin_ready")
        ss_ready, xn_ready, xT_psum, hT_ready = map(sem, ("ss_ready", "xn_ready", "xT_psum", "hT_ready"))
        hT_first, logitT_psum, logitT_ready = map(sem, ("hT_first", "logitT_psum", "logitT_ready"))
        gate_first_tile, half_squares, scaled = map(sem, ("gate_first_tile", "half_squares", "scaled"))
        scaled_gain = sem("scaled_gain")
        var_ready, mean_square, rstd_ready = sem("var_ready"), sem("mean_square"), sem("rstd_ready")
        read_dve, read_act = sem("read_dve"), sem("read_act")
        rotated, qkT_psum, qkT_ready, kz_ready = map(sem, ("rotated", "qkT_psum", "qkT_ready", "kz_ready"))
        ret_psum, scores_ready, kv_ready, ret_read = map(sem, ("ret_psum", "scores_ready", "kv_ready", "ret_read"))
        square_in, squared, sig_g = sem("square_in"), sem("squared"), sem("sig_g")
        pool_psum, mixT_ready, ypT_ready = map(sem, ("pool_psum", "mixT_ready", "ypT_ready"))
        yret_ready, yrT_psum, yrT_ready = map(sem, ("yret_ready", "yrT_psum", "yrT_ready"))
        branch_read, mT_psum, mT_ready, x_ready = map(sem, ("branch_read", "mT_psum", "mT_ready", "x_ready"))
        logits_psum, exp_in, exp_ready = map(sem, ("logits_psum", "exp_in", "exp_ready"))
        mask_ready, comb_ready, route_psum, route_ready = map(sem, ("mask_ready", "comb_ready", "route_psum", "route_ready"))
        bias_psum, bias_read, ple_read = map(sem, ("bias_psum", "bias_read", "ple_read"))
        pT_psum, pT_ready, ple_psum = sem("pT_psum"), sem("pT_ready"), sem("ple_psum")
        gate_sig, out_ready = sem("gate_sig"), sem("out_ready")

        first = ExpertSemaphores(sem, "first")
        more = ExpertSemaphores(sem, "more")
        used, loaded = first.chunk_used, first.loaded

        block = ctx.enter_context(nc.Block())

        def two_banks(b):
            return ps[:, b:b + 2, :].rearrange("p b n -> p (b n)")

        def bank_cols(b, n=KD):
            return ps[:, b, :].rearrange("p (k s) -> p k s", k=n)

        SUM_BANKS = (6, 7, 4, 5)

        def across(ap, n):
            return ap.unsqueeze(2).to_broadcast([P, ap.shape[1], n])

        def block_read(j):
            dve_blocks = [0, 1, 2, 3, 8, 9]
            if j in dve_blocks:
                return read_dve, 2 * (dve_blocks.index(j) + 1)
            act_blocks = [4, 5, 6, 7, 10, 11, 12, 13]
            return read_act, 2 * (act_blocks.index(j) + 1)

        def slot_of(c):
            return c % SLOTS

        PLE_LOADS = (PLE_CHUNK - EXTRAS) // SLOTS + 1
        assert (PLE_CHUNK - EXTRAS) % SLOTS >= 4

        PLACES = list(range(MIXER_SLOTS))
        for two in range(PIECES // 2):
            at = (PARTS * MIXER_BLOCKS - PIECES + 2 * two) % PIECES // 2
            PLACES += [MIXER_SLOTS + at, MIXER_SLOTS + PIECES // 2 + at]

        extra_places = (B[2][:, :], B[7][:, :], B[1][:, :], hT[:, :, :].rearrange("p k s -> p (k s)"), B[5][:, :])

        def is_extra(s, pair, c):
            return s is first and isinstance(pair, int) and pair == 0 and MIXER_SLOTS <= c < MIXER_SLOTS + EXTRAS

        def in_ring(s, pair, c):
            early = isinstance(pair, int) and pair == 0 and c < MIXER_SLOTS
            return c - EXTRAS if s is first and not early else c

        def slot(s, pair, c):
            if is_extra(s, pair, c):
                return extra_places[c - MIXER_SLOTS]
            return ring[:, PLACES[slot_of(in_ring(s, pair, c))], :]

        def signal(s, pair, c):
            if is_extra(s, pair, c):
                return extra_loaded[c - MIXER_SLOTS]
            return s.loaded[slot_of(in_ring(s, pair, c))]

        def piece_of(p):
            at = p // 2 - 2 * PLE_BLOCK if p >= PARTS * PLE_BLOCK else chunk_of(p) % MIXER_SLOTS
            return ring[:, at, (p % 2) * PIECE:(p % 2 + 1) * PIECE]

        def piece_loaded(eng, p):
            if p >= PARTS * PLE_BLOCK:
                eng.wait_ge(loaded[p // 2 - 2 * PLE_BLOCK], 16 * (PLE_LOADS + 1))
            else:
                c = chunk_of(p)
                eng.wait_ge(mixer_loaded[c % MIXER_SLOTS], 16 * (c // MIXER_SLOTS + 1))

        def expert_ready(eng, s, pair, h, i):
            c = 2 * i + h
            if is_extra(s, pair, c):
                eng.wait_ge(signal(s, pair, c), 16)
            else:
                eng.wait_ge(signal(s, pair, c), 16 * (in_ring(s, pair, c) // SLOTS + 1) + 32 * pair)

        left_body = {n: sem(f"left_body_{n}") for n in ("sp", "pe", "act", "dve")}

        def more_pairs(name, eng, body, skipped, before=None):
            top_count = eng.value_load(count_top[0:1, 0:1], min_val=0, max_val=SEQ)
            with eng.If(top_count > BLOCK):
                if before:
                    eng.wait_ge(*before)
                with eng.Fori(0, N_EXPERTS) as e:
                    for half in range(2):
                        low = (1 + 2 * half) * BLOCK
                        n_tokens = eng.value_load(counts[0:1, bass.ds(e, 1)], min_val=0, max_val=SEQ)
                        with eng.If(n_tokens > low):
                            body(2 * e + half, e, low)
                            eng.sem_inc(left_body[name], 1)
                        with eng.Else():
                            skipped()
                        eng.nop()
                eng.nop()
            eng.nop()

        @block.sync
        def _(sp):
            def load(c, src, k):
                if c >= MIXER_SLOTS:
                    former = c - MIXER_SLOTS
                    if former == POOL_CHUNK:
                        sp.wait_ge(pool_projected, 4)
                    else:
                        sp.wait_ge(lo_ready, 2 * (former - (former > POOL_CHUNK)) + 2)
                dst = ring[:, c % MIXER_SLOTS, :].rearrange("p (k n) -> p k n", k=k)
                sp.dma_start(dst, src).then_inc(mixer_loaded[c % MIXER_SLOTS], 16)

            for i in range(TILES):
                sp.dma_start(x[:, i, :], t["x"][0, i * P:(i + 1) * P, :]).then_inc(x_loaded[i], 16)
            for i, g in enumerate((t["g_mix_norm"], t["g_ret_norm"], t["pool_scale"], t["g_ffn_norm"], t["g_ple_norm"])):
                sp.dma_start(vec_rows[KD * i:KD * (i + 1), :], g[0].rearrange("(k p) -> k p", p=P)).then_inc(vec_loaded, 16)
            sp.dma_start(pos_int, t["positions"][0].rearrange("(i p) -> i p", p=P)).then_inc(vec_loaded, 16)
            w_in = t["w_in"][0].rearrange("(k p) n -> p k n", p=P)
            chunk = 0
            for j, cb in enumerate(COLUMN_BLOCKS):
                if j == POOL_AFTER:
                    load(chunk, t["w_pool"][0].rearrange("g (k p) n -> p (g k) n", p=P), 8)
                    chunk += 1
                for half in range(2):
                    load(chunk, w_in[:, 4 * half:4 * half + 4, cb * N:(cb + 1) * N], 4)
                    chunk += 1
            for unit in range(4):
                w = t["w_branch"][0, 1 - unit % 2].rearrange("(k p) n -> p k n", p=P)
                for half in range(2):
                    load(chunk, w[:, 4 * half:4 * half + 4, (unit // 2) * N:(unit // 2 + 1) * N], 4)
                    chunk += 1
            w_out = t["w_out"][0].rearrange("(k p) n -> p k n", p=P)
            for half in range(2):
                for n in range(2):
                    load(chunk, w_out[:, 4 * half:4 * half + 4, n * N:(n + 1) * N], 4)
                    chunk += 1
            assert chunk == MIXER_CHUNKS

            def load_expert(s, pair, c, e):
                i = c // 2
                dst = slot(s, pair, c)
                if i < UP_CHUNKS:
                    src = t["w_gate_up"][0, bass.ds(e, 1), i * P:(i + 1) * P, :].rearrange("e p n -> p (e n)")
                else:
                    r = (i - UP_CHUNKS) * 2 * P
                    src = t["w_down"][0, bass.ds(e, 1), r:r + 2 * P, :].rearrange("e (k p) n -> p (e k) n", p=P)
                    dst = dst.rearrange("p (k n) -> p k n", k=2)
                sp.dma_start(dst, src).then_inc(signal(s, pair, c), 16)

            def load_early(c):
                former = MIXER_CHUNKS - 1 - (MIXER_CHUNKS - 1 - c) % MIXER_SLOTS
                sp.wait_ge(lo_ready, 2 * (former - 1) + 2)
                load_expert(first, 0, c, c % 2)

            load_early(5)
            sp.wait_ge(piece_used, PARTS * (BRANCH + 3))
            load_expert(first, 0, 6, 0)
            load_early(0)
            load_early(1)
            sp.wait_ge(branch_read, 3)
            load_expert(first, 0, 7, 1)
            load_early(2)
            load_early(3)
            sp.wait_ge(branch_read, 4)
            for row in range(2):
                sp.dma_start(bias_rows_first[row:row + 1, :], t["b_gate_up"][0, row:row + 1, :]).then_inc(first.bias_loaded, 16)
            sp.wait_ge(mT_psum, 4)
            load_expert(first, 0, 8, 0)
            load_early(4)
            for c in range(MIXER_SLOTS + EXTRAS, PER_PAIR):
                at = in_ring(first, 0, c)
                if at < SLOTS:
                    sp.wait_ge(piece_used, PARTS * MIXER_BLOCKS - PIECES + 2 * ((at - MIXER_SLOTS) // 2) + 2)
                else:
                    former = at - SLOTS
                    sp.wait_ge(used, (former if former < MIXER_SLOTS else former + EXTRAS) + 1)
                load_expert(first, 0, c, c % 2)
                if at == SLOTS - 1:
                    load_expert(first, 0, 10, 0)
                    sp.wait_ge(logitT_psum, 1)
                    load_expert(first, 0, 9, 1)

            with sp.Fori(1, PAIRS) as pair:
                for c in range(PER_PAIR):
                    sp.wait_ge(used, PER_PAIR * pair + c - SLOTS + 1)
                    load_expert(first, pair, c, 2 * pair + c % 2)

            def body(j, e, low):
                for c in range(PER_PAIR):
                    if c >= SLOTS:
                        sp.wait_ge(more.chunk_used, PER_PAIR * j + c - SLOTS + 1)
                    load_expert(more, j, c, e)
                sp.wait_ge(more.pair_done, j + 1)

            def skipped():
                for s in range(SLOTS):
                    sp.sem_inc(more.loaded[s], 32)

            sp.wait_ge(route_ready, 1)
            more_pairs("sp", sp, body, skipped, before=(used, PLE_CHUNK))
            w_gate = t["w_ple_gate"][0].rearrange("(k p) n -> p k n", p=P)
            for n in range(2):
                for half in range(2):
                    at = 2 * n + half
                    sp.wait_ge(used, SLOTS * (PLE_LOADS - 1) + at + EXTRAS + 1)
                    sp.dma_start(ring[:, at, :].rearrange("p (k n) -> p k n", k=4),
                                 w_gate[:, 4 * half:4 * half + 4, n * N:(n + 1) * N]).then_inc(loaded[at], 16)
            for i in range(TILES):
                sp.wait_ge(scaled, i + 1)
                sp.wait_ge(out_ready, i + 1)
                sp.dma_start(t["y"][0, i * P:(i + 1) * P, :], result[:, i, :]).then_inc(stored, 16)
            sp.wait_ge(stored, 16 * TILES)

        @block.tensor
        def _(pe):
            def mm(out, lhsT, rhs, start, stop):
                return pe.matmul(out, lhsT, rhs, start=start, stop=stop, skip_group_check=True)

            def transpose_bank(src, bank, j, done):
                for kk in range(2):
                    for i in range(TILES):
                        c = 2 * j + kk
                        last = pe.transpose(ps[:, bank, kk * SEQ + i * P:kk * SEQ + (i + 1) * P],
                                            src[:, i, c * P:(c + 1) * P], ident)
                last.then_inc(done, 1)

            def transpose16(src, done, free=None):
                for j in range(KD // 2):
                    if free:
                        semaphore, value, per_bank = free
                        pe.wait_ge(semaphore, value + per_bank * j)
                    transpose_bank(src, 4 + j, j, done)

            def products(piece, part, i, parts, n_bank):
                hi, lo = parts
                at = piece % PIECES
                out, tokens = ps[:, n_bank + i, :], slice(i * P, (i + 1) * P)
                for kk in range(2):
                    c, columns = 2 * part + kk, slice(kk * N, (kk + 1) * N)
                    mm(out, hi[:, c, tokens], w_hi[:, at, columns], c == 0, False)
                    mm(out, hi[:, c, tokens], w_lo[:, at, columns], False, False)
                    last = mm(out, lo[:, c, tokens], w_hi[:, at, columns], False, c == KD - 1)
                return last

            def project(block, parts, n_bank, ready=None):
                for part in range(PARTS):
                    if ready:
                        pe.wait_ge(*ready(part))
                    pe.wait_ge(lo_ready, PARTS * block + part + 1)
                    products(PARTS * block + part, part, 0, parts, n_bank)
                    products(PARTS * block + part, part, 1, parts, n_bank).then_inc(piece_used, 1)

            def project_by_tile(block, parts, n_bank, first_done):
                for part in range(PARTS):
                    pe.wait_ge(lo_ready, PARTS * block + part + 1)
                    last = products(PARTS * block + part, part, 0, parts, n_bank)
                last.then_inc(first_done, 1)
                for part in range(PARTS):
                    products(PARTS * block + part, part, 1, parts, n_bank).then_inc(piece_used, 1)

            def up_bias(s, pair, banks=range(4), rows=bias_rows):
                pe.wait_ge(s.bias_loaded, 32 * pair + 32)
                for n in banks:
                    mm(ps[:, n, :], const[0:2, SEL:SEL + P], rows[:, n * N:(n + 1) * N], True, False)

            pe.wait_ge(early_loaded, 16)
            for i in range(TILES):
                pe.wait_ge(x_loaded[i], 16)
            for j in range(2):
                transpose_bank(x, 4 + j, j, xT_psum)
            pe.wait_ge(vec_loaded, 16 * 6)
            pe.transpose(ps[:, 0, 0:5 * KD], vec_rows, ident[0:5 * KD, 0:5 * KD])
            pe.wait_ge(pos_cast, 1)
            pe.transpose(ps[:, 0, 64:64 + TILES], pos_row, ident[0:TILES, 0:TILES]).then_inc(vec_psum, 1)
            for j in range(2, 4):
                transpose_bank(x, 4 + j, j, xT_psum)

            def column_block(j):
                if j == 0:
                    pe.wait_ge(vecs_read, 1)
                if j >= 2:
                    pe.wait_ge(*block_read(j - 2))
                project(j, hT_parts, 2 * (j % 2), (lambda part: (hT_ready, 2 * part + 2)) if j == 0 else None)

            def scores(g):
                if g == 0:
                    pe.wait_ge(qkT_ready, 8)
                    pe.wait_ge(kz_ready, 1)
                    pe.wait_ge(read_act, 2 * 2)
                else:
                    pe.wait_ge(ret_read, g)
                for c in range(TILES):
                    for i in range(4):
                        h = 4 * g + i
                        last = mm(ps[:, 4 + c, i * P:(i + 1) * P], kT[:, h, c * P:(c + 1) * P],
                                  qT[:, h, c * P:(c + 1) * P], True, True)
                    last.then_inc(ret_psum, 1)
                if g:
                    pe.wait_ge(kv_ready, g)
                for i in range(4):
                    h = 4 * g + i
                    last = mm(ps[:, 6, i * P:(i + 1) * P], k[:, 0, h * P:(h + 1) * P],
                              v[:, 0, h * P:(h + 1) * P], True, True)
                last.then_inc(ret_psum, 1)

            def inner(g):
                pe.wait_ge(scores_ready, 2 * g + 2)
                for c in range(TILES):
                    for i in range(4):
                        h = 4 * g + i
                        last = mm(ps[:, 4 + c, i * P:(i + 1) * P], scoresT[:, c, i * P:(i + 1) * P],
                                  v[:, c, h * P:(h + 1) * P], True, True)
                last.then_inc(ret_psum, 1)
                pe.wait_ge(kv_ready, g + 1)
                for i in range(4):
                    h = 4 * g + i
                    last = mm(ps[:, 7, i * P:(i + 1) * P], qT[:, h, P:2 * P], kv[:, i * P:(i + 1) * P], True, True)
                last.then_inc(ret_psum, 1)

            def pool_mix():
                pe.wait_ge(ret_read, 2)
                for j in range(4):
                    for kk in range(2):
                        c = 2 * j + kk
                        m = POOLM + 3 * P * (c // 2)
                        out = ps[:, 4 + j, kk * SEQ:(kk + 1) * SEQ]
                        uc = [u[:, i, c * P:(c + 1) * P] for i in range(TILES)]
                        mm(out[:, 0:P], uc[0], const[:, m:m + P], True, True)
                        mm(out[:, P:2 * P], uc[0], const[:, m + P:m + 2 * P], True, False)
                        last = mm(out[:, P:2 * P], uc[1], const[:, m + 2 * P:m + 3 * P], False, True)
                    last.then_inc(pool_psum, 1)

            def pool_project():
                pe.wait_ge(mixT_ready, 4)
                pe.wait_ge(mixer_loaded[POOL_CHUNK % MIXER_SLOTS], 16 * (POOL_CHUNK // MIXER_SLOTS + 1))
                w = ring[:, POOL_CHUNK % MIXER_SLOTS, :].rearrange("p (k n) -> p k n", k=8)
                for m in range(KD):
                    for kk in range(2):
                        last = mm(ps[:, 4 + m // 2, (m % 2) * SEQ:(m % 2 + 1) * SEQ],
                                  w[:, 2 * (m // 2) + kk, (m % 2) * P:(m % 2 + 1) * P],
                                  mixedT[:, 2 * (m // 2) + kk, :], kk == 0, kk == 1)
                    if m % 2:
                        last.then_inc(pool_projected, 1)

            for j in range(4):
                column_block(j)
            pe.wait_ge(const_loaded, 16)
            column_block(4)
            pe.wait_ge(rotated, 4)
            transpose16(q, qkT_psum)
            column_block(5)
            pe.wait_ge(rotated, 8)
            transpose16(k, qkT_psum, free=(qkT_ready, 1, 1))
            column_block(6)
            scores(0)
            column_block(7)
            inner(0)
            column_block(8)
            scores(1)
            column_block(9)
            inner(1)
            column_block(10)
            pool_mix()
            column_block(11)
            pool_project()
            column_block(12)
            column_block(13)
            pe.wait_ge(yret_ready, 1)
            transpose16(ret, yrT_psum, free=(ypT_ready, 2, 2))

            def merged_to_width(half):
                pe.wait_ge(branch_read, 2 * half + 2)
                for j in (2 * half, 2 * half + 1):
                    transpose_bank(merged, 4 + j, j, mT_psum)

            for unit in range(4):
                if unit < 2:
                    pe.wait_ge(*block_read(12 + unit))
                else:
                    pe.wait_ge(branch_read, unit - 1)
                if unit == 0:
                    pe.wait_ge(ypT_ready, KD)
                project(BRANCH + unit, yretT_parts if unit % 2 else ypoolT_parts, 2 * (unit % 2),
                        (lambda part: (yrT_ready, 2 * part + 2)) if unit == 1 else None)
                if unit == 2:
                    merged_to_width(0)

            for turn in range(4):
                half, n = turn // 2, turn % 2
                for which in range(2):
                    part, piece = 2 * half + which, PARTS * OUT + 2 * turn + which
                    pe.wait_ge(mT_ready, part + 1)
                    pe.wait_ge(lo_ready, piece + 1)
                    products(piece, part, 0, mergedT_parts, 2 * n)
                    products(piece, part, 1, mergedT_parts, 2 * n).then_inc(piece_used, 1)
                if turn == 0:
                    merged_to_width(1)

            pe.wait_ge(mT_ready, 4)
            pe.wait_ge(x_ready, TILES)
            for j in range(2):
                transpose_bank(x, 4 + j, j, xT_psum)
            pe.wait_ge(x_ready, 2 * TILES)
            for j in range(2, 4):
                transpose_bank(x, 4 + j, j, xT_psum)
            pe.wait_ge(router_loaded, 32)
            for c in range(KD):
                if c < 4:
                    pe.wait_ge(hT_first, c + 1)
                if c >= 4 and c % 2 == 0:
                    pe.wait_ge(hT_ready, KD + c // 2 - 1)
                last = mm(ps[0:N_EXPERTS, 0, 0:SEQ], w_router[:, c, :], hT[:, c, :], c == 0, c == KD - 1)
            last.then_inc(logitT_psum, 1)
            pe.wait_ge(logitT_ready, 1)
            for i in range(TILES):
                last = pe.transpose(ps[:, 6, i * N_EXPERTS:(i + 1) * N_EXPERTS], logitT[:, i * P:(i + 1) * P],
                                    ident[0:N_EXPERTS, 0:N_EXPERTS])
            last.then_inc(logits_psum, 1)
            up_bias(first, 0, range(0, 3), bias_rows_first)
            pe.wait_ge(mask_ready, 1)
            mm(ps[:, 4, 0:2 * N_EXPERTS], tri, mask_flat, True, False)
            mm(ps[:, 4, N_EXPERTS:2 * N_EXPERTS], ones, mask[:, 0, :], False, True).then_inc(route_psum, 1)
            up_bias(first, 0, range(3, 4), bias_rows_first)

            def gather(s, pair):
                pe.wait_ge(s.onehot_ready, pair + 1)
                for c in range(KD // 2):
                    for i in range(TILES):
                        for b in range(2):
                            k = 4 * b + c
                            last = mm(ps[:, 6 + b, c * P:(c + 1) * P], xn[:, i, k * P:(k + 1) * P],
                                      onehot[:, i, :], i == 0, i == TILES - 1)
                last.then_inc(s.gathered, 1)

            def both(s, pair, i, lhsT, c, columns, bank, start, stop):
                for n in range(len(columns)):
                    for h in range(2):
                        w = slot(s, pair, 2 * i + h)[:, columns[n]:columns[n] + N]
                        last = mm(ps[h * BLOCK:(h + 1) * BLOCK, bank + n, :], lhsT[:, c, h * BLOCK:(h + 1) * BLOCK],
                                  w, start, stop)
                        if columns[n] + N == SLOT:
                            last.then_inc(s.chunk_used, 1)

            def gate_up(s, pair):
                for i in range(UP_CHUNKS):
                    if i % 4 == 0:
                        pe.wait_ge(s.hg_ready, 2 * pair + 1 + i // 4)
                    for h in range(2):
                        expert_ready(pe, s, pair, h, i)
                    both(s, pair, i, hg, i, [n * N for n in range(4)], 0, False, i == UP_CHUNKS - 1)

            def act_to_width(s, pair):
                for half in range(2):
                    pe.wait_ge(s.act_ready, 2 * pair + half + 1)
                    for quarter in range(4):
                        c = 4 * half + quarter
                        last = pe.transpose(ps[:, half, quarter * P:(quarter + 1) * P], gate[:, c * P:(c + 1) * P], ident)
                    last.then_inc(s.act_xposed, 1)

            def down(s, pair, bank=4):
                for i in range(DOWN_CHUNKS):
                    if i % 2 == 0:
                        pe.wait_ge(s.actT_ready, 2 * pair + 1 + i // 2)
                    for h in range(2):
                        expert_ready(pe, s, pair, h, UP_CHUNKS + i)
                    for kk in range(2):
                        c = 2 * i + kk
                        both(s, pair, UP_CHUNKS + i, actT, c, [kk * D, kk * D + N], bank, c == 0, c == KD - 1)

            def scatter_weights(s, pair):
                pe.wait_ge(s.sw_ready, pair + 1)
                pe.wait_ge(s.up_read, pair + 1)
                for i in range(TILES):
                    last = pe.transpose(ps[:, 2, i * P:(i + 1) * P], weighted[:, i, :], ident)
                last.then_inc(s.swt_done, 1)

            def scatter(s, pair):
                pe.wait_ge(s.st_ready, pair + 1)
                pe.wait_ge(s.os_ready, pair + 1)
                for i in range(4):
                    n, tile = i // 2, i % 2
                    mm(ps[:, SUM_BANKS[i], :], scatterT[:, tile * P:(tile + 1) * P],
                       slot_rows[:, n * N:(n + 1) * N], True, True).then_inc(s.scattered, 1)

            def project_ple():
                pe.wait_ge(first.os_ready, REST_PAIR + 1)
                pe.wait_ge(p_loaded, 16)
                pe.wait_ge(proj_loaded, 16)
                for c in range(2):
                    for i in range(TILES):
                        last = pe.transpose(ps[:, 4, c * SEQ + i * P:c * SEQ + (i + 1) * P],
                                            p_in[:, i, c * P:(c + 1) * P], ident)
                last.then_inc(pT_psum, 1)
                pe.wait_ge(pT_ready, 1)
                for i in range(4):
                    n, tile = i // 2, i % 2
                    if i == 1:
                        pe.wait_ge(route_ready, 1)
                    for c in range(2):
                        last = mm(ps[:, SUM_BANKS[i], :], pT[:, c, tile * P:(tile + 1) * P],
                                  w_proj[:, c, n * N:(n + 1) * N], c == 0, c == 1)
                    last.then_inc(ple_psum, 1)

            def route_rest():
                pe.wait_ge(comb_ready, 1)
                pe.wait_ge(first.hg_ready, 2 * (REST_PAIR + 2))
                for i in range(TILES):
                    pe.transpose(ps[0:N_EXPERTS, 7, i * P:(i + 1) * P], comb[:, i, 0:N_EXPERTS], ident)
                for i in range(TILES):
                    last = mm(ps[0:1, 7, SEQ:SEQ + N_EXPERTS], ones[:, 0:1], mask[:, i, :], i == 0, i == TILES - 1)
                last.then_inc(route_psum, 1)

            def output_bias():
                pe.wait_ge(late_loaded, 32)
                for i in range(4):
                    n, tile = i // 2, i % 2
                    pe.wait_ge(ple_read, i + 1)
                    mm(ps[:, SUM_BANKS[i], :], combT[:, tile * P:(tile + 1) * P], b_down[:, n * N:(n + 1) * N],
                       True, True).then_inc(bias_psum, 1)

            def pair_steps(pair, is_first=False, is_last=False, has_rest=False):
                if not is_first:
                    pe.wait_ge(first.st_ready, pair)
                    up_bias(first, pair)
                gate_up(first, pair)
                if not is_first:
                    scatter(first, pair - 1)
                    scatter_weights(first, pair)
                    act_to_width(first, pair)
                    if not is_last:
                        pe.wait_ge(first.acc_done, 4 * pair - 2)
                        gather(first, pair + 1)
                else:
                    gather(first, 1)
                    scatter_weights(first, 0)
                    act_to_width(first, 0)
                if is_last:
                    pe.wait_ge(first.acc_done, 4 * pair - 2)
                elif not is_first:
                    pe.wait_ge(first.acc_done, 4 * pair)
                down(first, pair, 6 if is_last else 4)
                if has_rest:
                    route_rest()
                    project_ple()
                    output_bias()
                    pe.wait_ge(bias_read, 4)

            pe.wait_ge(xn_ready, TILES)
            gather(first, 0)
            pair_steps(0, is_first=True)
            with pe.Fori(1, REST_PAIR) as pair:
                pair_steps(pair)
            pair_steps(REST_PAIR, has_rest=True)
            with pe.Fori(REST_PAIR + 1, PAIRS - 1) as pair:
                pair_steps(pair)
            pair_steps(PAIRS - 1, is_last=True)
            pe.wait_ge(first.acc_done, 4 * (PAIRS - 1))
            scatter(first, PAIRS - 1)

            def body(j, e, low):
                pe.wait_ge(first.acc_done, 4 * PAIRS)
                gather(more, j)
                up_bias(more, j)
                gate_up(more, j)
                scatter_weights(more, j)
                act_to_width(more, j)
                down(more, j)
                scatter(more, j)
                pe.wait_ge(more.pair_done, j + 1)

            def skipped():
                for s, n in ((more.gathered, 1), (more.chunk_used, PER_PAIR), (more.swt_done, 1),
                             (more.act_xposed, 2), (more.scattered, 4)):
                    pe.sem_inc(s, n)

            more_pairs("pe", pe, body, skipped)

            pe.wait_ge(x_ready, 2 * TILES + 4)
            for j in range(4):
                transpose_bank(x, j, j, xT_psum)
            project(PLE_BLOCK, hT_parts, 4, lambda part: (hT_ready, KD + 2 + 2 * part + 2))
            project_by_tile(PLE_BLOCK + 1, hT_parts, 6, gate_first_tile)

        @block.gpsimd
        def _(pool):
            own = [0]

            def step(ins):
                own[0] += 1
                ins.then_inc(mean_square, 1)
                pool.wait_ge(mean_square, own[0])

            def root(dst, src, n, eps):
                step(nc.gpsimd.tensor_scalar(dst, src, 1.0 / n, eps, ALU.mult, ALU.add))
                nc.gpsimd.tensor_tensor(dst, dst, exponent[:, 0:dst.shape[1]], ALU.pow).then_inc(rstd_ready, 1)

            step(nc.gpsimd.memset(exponent, -0.5))
            pool.wait_ge(ss_ready, TILES)
            root(rstd, ss, D, RMS_EPS)
            pool.wait_ge(var_ready, 1)
            root(var, var, P, GN_EPS)
            for turn in range(2):
                pool.wait_ge(ss_ready, TILES * (turn + 2))
                root(rstd, ss, D, RMS_EPS)
            for i in range(TILES):
                pool.wait_ge(half_squares, TILES + i + 1)
                step(nc.gpsimd.tensor_tensor(ss[:, i:i + 1], ss_half[:, 0, i:i + 1], ss_half[:, 1, i:i + 1], ALU.add))
                root(rstd[:, i:i + 1], ss[:, i:i + 1], D, RMS_EPS)

        @block.scalar
        def _(act_eng):
            e = act_eng
            e.dma_start(const[:, 0:EARLY], t["const"][:, 0:EARLY]).then_inc(early_loaded, 16)

            split = [0]

            def split_hi(end):
                for p in range(split[0], end):
                    if p % 2 == 0:
                        piece_loaded(e, p)
                    if p >= PIECES:
                        e.wait_ge(piece_used, p - PIECES + 1)
                    nc.scalar.copy(w_hi[:, p % PIECES, :], piece_of(p)).then_inc(hi_ready, 1)
                split[0] = max(end, split[0])

            def high(parts, psum, n, g, done, bank=4, blocks=range(KD)):
                for c in blocks:
                    if c % 2 == 0:
                        e.wait_ge(psum, n + c // 2 + 1)
                    nc.scalar.activation(parts[0][:, c, :], ps[:, bank + c // 2, (c % 2) * SEQ:(c % 2 + 1) * SEQ], ACT.Copy,
                                         scale=vecs[:, g + c:g + c + 1]).then_inc(done, 1)

            e.wait_ge(vecs_read, 1)
            high(hT_parts, xT_psum, 0, G_MIX, hT_hi, 4, range(0, 4))
            split_hi(1)
            high(hT_parts, xT_psum, 0, G_MIX, hT_hi, 4, range(4, KD))
            split_hi(4)
            e.dma_start(const[:, EARLY:], t["const"][:, EARLY:]).then_inc(const_loaded, 16)
            split_hi(ahead(-1))
            for i in range(TILES):
                e.wait_ge(x_loaded[i], 16)
                if i:
                    e.wait_ge(ss_ready, i)
                nc.scalar.activation(scratch, x[:, i, :], ACT.Square, accum_out=ss[:, i:i + 1]).then_inc(ss_ready, 1)
            e.wait_ge(angles_ready, 1)
            nc.scalar.activation(sin, angle, ACT.Sin).then_inc(sin_ready, 1)
            nc.scalar.activation(cos, turns, ACT.Sin).then_inc(sin_ready, 1)

            def copies_qk(n):
                for j in range(4):
                    e.wait_ge(qkT_psum, 4 * n + j + 1)
                    nc.scalar.copy((qT, kT)[n][:, 2 * j:2 * j + 2, :], bank_cols(4 + j, 2)).then_inc(qkT_ready, 1)

            def read_block(j, dst, func):
                n = j % 2
                split_hi(ahead(j))
                e.wait_ge(piece_used, PARTS * (j + 1))
                for i in range(TILES):
                    nc.scalar.activation(dst[:, i, n * N:(n + 1) * N], ps[:, 2 * n + i, :], func,
                                         scale=rstd[:, i:i + 1]).then_inc(read_act, 1)

            def read_kv(g):
                e.wait_ge(ret_psum, 5 * g + 3)
                nc.scalar.copy(kv, ps[:, 6, :]).then_inc(kv_ready, 1)

            for j in range(4):
                split_hi(ahead(j))
            e.wait_ge(rstd_ready, 1)
            read_block(4, v, ACT.Copy)
            copies_qk(0)
            read_block(5, v, ACT.Copy)
            copies_qk(1)
            e.wait_ge(rotated, 8)
            read_block(6, u, ACT.Copy)
            read_kv(0)
            read_block(7, u, ACT.Copy)

            def silu_block(j):
                n = j % 2
                split_hi(ahead(j))
                e.wait_ge(piece_used, PARTS * (j + 1))
                for i in range(TILES):
                    nc.scalar.activation(silu_g[:, i, n * N:(n + 1) * N], ps[:, 2 * n + i, :], ACT.Sigmoid,
                                         scale=rstd[:, i:i + 1]).then_inc(sig_g, 1)

            silu_block(8)
            e.wait_ge(ret_read, 1)
            read_kv(1)
            silu_block(9)
            e.wait_ge(ret_read, 2)
            e.wait_ge(square_in, 1)
            nc.scalar.activation(square, ret, ACT.Square).then_inc(squared, 1)
            read_block(10, gates[0], ACT.Sigmoid)
            for j in range(4):
                e.wait_ge(pool_psum, j + 1)
                nc.scalar.copy(mixedT[:, 2 * j:2 * j + 2, :], bank_cols(4 + j, 2)).then_inc(mixT_ready, 1)
            e.dma_start(b_down, t["b_down"][0]).then_inc(late_loaded, 16)
            e.dma_start(g_final, t["g_final"].unsqueeze(0).to_broadcast([P, D])).then_inc(late_loaded, 16)
            read_block(11, gates[0], ACT.Sigmoid)
            high(ypoolT_parts, pool_projected, 0, G_POOL, ypT_hi)
            read_block(12, gates[1], ACT.Sigmoid)
            read_block(13, gates[1], ACT.Sigmoid)
            high(yretT_parts, yrT_psum, 0, G_RET, yrT_hi)
            for j in range(4):
                split_hi(ahead(BRANCH + 2) if j < 2 else ahead(OUT))
                e.wait_ge(mT_psum, j + 1)
                nc.scalar.copy(mergedT_parts[0][:, 2 * j:2 * j + 2, :], bank_cols(4 + j, 2)).then_inc(mT_hi, 1)
            e.wait_ge(branch_read, 4)
            e.dma_start(w_router, t["w_router"][0].rearrange("(k p) n -> p k n", p=P)).then_inc(router_loaded, 16)
            e.dma_start(b_router, t["b_router"].to_broadcast([P, N_EXPERTS])).then_inc(router_loaded, 16)
            e.dma_start(w_proj, t["w_ple_proj"][0].rearrange("(c p) n -> p c n", p=P)).then_inc(proj_loaded, 16)
            e.dma_start(p_in, t["p"][0, 0].rearrange("(i p) n -> p i n", p=P)).then_inc(p_loaded, 16)

            def load_bias(s, experts):
                for h, ex in enumerate(experts):
                    e.dma_start(bias_rows[h:h + 1, :], t["b_gate_up"][0, bass.ds(ex, 1), :]).then_inc(s.bias_loaded, 16)

            for c in range(4):
                if c % 2 == 0:
                    e.wait_ge(xT_psum, 4 + c // 2 + 1)
                nc.scalar.activation(hT[:, c, :], ps[:, 4 + c // 2, (c % 2) * SEQ:(c % 2 + 1) * SEQ], ACT.Copy,
                                     scale=vecs[:, G_FFN + c:G_FFN + c + 1]).then_inc(hT_first, 1)
            for i in range(TILES):
                e.wait_ge(x_ready, TILES + i + 1)
                nc.scalar.activation(xn[:, i, :], x[:, i, :], ACT.Square,
                                     accum_out=ss[:, i:i + 1]).then_inc(ss_ready, 1)
            e.wait_ge(rstd_ready, 3)
            for i in range(TILES):
                nc.scalar.activation(xn[:, i, :], x[:, i, :], ACT.Copy, scale=rstd[:, i:i + 1]).then_inc(xn_ready, 1)
            e.wait_ge(exp_in, 1)
            for i in range(TILES):
                nc.scalar.activation(expo[:, i, :], logit[:, i, 0:N_EXPERTS], ACT.Exp,
                                     bias=neg[:, i:i + 1]).then_inc(exp_ready, 1)

            def sigmoid(s, pair):
                e.wait_ge(s.gate_ready, pair + 1)
                nc.scalar.activation(sig, gate, ACT.Sigmoid, scale=ALPHA).then_inc(s.sig_ready, 1)

            def read_actT(s, pair):
                for half in range(2):
                    e.wait_ge(s.act_xposed, 2 * pair + half + 1)
                    nc.scalar.copy(B[2][:, half * N:(half + 1) * N], ps[:, half, :]).then_inc(s.actT_ready, 1)

            def read_down(s, pair, bank=4):
                e.wait_ge(s.chunk_used, PER_PAIR * pair + PER_PAIR)
                nc.scalar.copy(slot_rows, two_banks(bank)).then_inc(s.os_ready, 1)

            sigmoid(first, 0)
            load_bias(first, (2, 3))
            read_actT(first, 0)
            read_down(first, 0)

            def inner_pair(pair):
                sigmoid(first, pair)
                load_bias(first, (2 * pair + 2, 2 * pair + 3))
                read_actT(first, pair)
                read_down(first, pair)

            with e.Fori(1, REST_PAIR) as pair:
                inner_pair(pair)
            inner_pair(REST_PAIR)
            e.wait_ge(pT_psum, 1)
            nc.scalar.copy(pT, bank_cols(4, 2)).then_inc(pT_ready, 1)
            with e.Fori(REST_PAIR + 1, PAIRS - 1) as pair:
                inner_pair(pair)
            sigmoid(first, PAIRS - 1)
            read_actT(first, PAIRS - 1)
            read_down(first, PAIRS - 1, 6)

            def body(j, ex, low):
                e.wait_ge(first.scattered, 4 * PAIRS)
                load_bias(more, (ex, ex))
                sigmoid(more, j)
                read_actT(more, j)
                read_down(more, j)
                e.wait_ge(more.pair_done, j + 1)

            def skipped():
                for s, n in ((more.bias_loaded, 32), (more.sig_ready, 1), (more.actT_ready, 2), (more.os_ready, 1)):
                    e.sem_inc(s, n)

            more_pairs("act", e, body, skipped)
            e.wait_ge(used, PLE_CHUNK)
            split_hi(PARTS * PLE_BLOCK + PARTS)
            high(hT_parts, xT_psum, 8, G_PLE, hT_hi, bank=0)
            split_hi(PARTS * PLE_BLOCK + PARTS + 1)
            for i in range(TILES):
                if i:
                    e.wait_ge(ss_ready, 2 * TILES + i)
                nc.scalar.activation(slot_rows, x[:, i, :], ACT.Square, accum_out=ss[:, i:i + 1]).then_inc(ss_ready, 1)
            split_hi(PARTS * PLE_BLOCK + 2 * PARTS)
            e.wait_ge(rstd_ready, 4)

            def gate_half(n, i):
                if n and i == 0:
                    e.wait_ge(gate_first_tile, 1)
                else:
                    e.wait_ge(piece_used, PARTS * (PLE_BLOCK + n + 1))
                nc.scalar.activation(ple_gate[:, n, i, :], ps[:, 4 + 2 * n + i, :], ACT.Sigmoid,
                                     scale=rstd[:, i:i + 1]).then_inc(gate_sig, 1)

            def square_half(n, i):
                e.wait_ge(x_ready, 2 * TILES + 4 + 2 * n + i + 1)
                if n or i:
                    e.wait_ge(half_squares, 2 * n + i)
                nc.scalar.activation(slot_rows[:, 0:N], x[:, i, n * N:(n + 1) * N], ACT.Square,
                                     accum_out=ss_half[:, n, i:i + 1]).then_inc(half_squares, 1)

            def scale_first(i):
                e.wait_ge(scaled_gain, i + 1)
                e.wait_ge(rstd_ready, 5 + i)
                nc.scalar.activation(result[:, i, 0:N], result[:, i, 0:N], ACT.Copy, scale=rstd[:, i:i + 1]).then_inc(scaled, 1)

            gate_half(0, 0)
            gate_half(0, 1)
            square_half(0, 0)
            square_half(0, 1)
            for i in range(TILES):
                gate_half(1, i)
                square_half(1, i)
                scale_first(i)

        @block.vector
        def _(dve):
            ve = nc.vector
            counts_of = {}

            order = [vec_order]

            def step(ins, s=None):
                s = s or order[0]
                c = counts_of.setdefault(id(s), Count())
                ins.then_inc(s, 1)
                c.n += 1
                dve.wait_ge(s, c.value())

            def own(s):
                return counts_of.setdefault(id(s), Count())

            dve.wait_ge(vec_loaded, 16 * 6)
            step(ve.tensor_copy(pos_row, pos_int), pos_cast)
            dve.wait_ge(vec_psum, 1)
            step(ve.tensor_copy(vecs[:, :], ps[:, 0, 0:5 * KD]))
            step(ve.tensor_copy(pos, ps[:, 0, 64:64 + TILES]), vecs_read)

            def post(ins, s):
                counts_of.setdefault(id(s), Count()).n += 1
                ins.then_inc(s, 1)

            split = [0]

            def split_lo(end):
                for p in range(split[0], end):
                    dve.wait_ge(hi_ready, p + 1)
                    post(ve.tensor_tensor(w_lo[:, p % PIECES, :], piece_of(p), w_hi[:, p % PIECES, :].bitcast(F32),
                                          ALU.subtract), lo_ready)
                split[0] = max(end, split[0])

            def low(parts, g, high, n, done, bank=4, blocks=range(KD)):
                for c in blocks:
                    if c % 2 == 0:
                        dve.wait_ge(high, n + c + 2)
                    post(ve.scalar_tensor_tensor(parts[1][:, c, :], ps[:, bank + c // 2, (c % 2) * SEQ:(c % 2 + 1) * SEQ],
                                                 vecs[:, g + c:g + c + 1], parts[0][:, c, :].bitcast(F32),
                                                 ALU.mult, ALU.subtract), done)

            low(hT_parts, G_MIX, hT_hi, 0, hT_ready, 4, range(0, 4))
            split_lo(1)
            low(hT_parts, G_MIX, hT_hi, 0, hT_ready, 4, range(4, KD))
            split_lo(ahead(-1))
            for i in range(TILES):
                step(ve.tensor_scalar(cos[:, i, :], const[:, INVF:INVF + 64], pos[:, i:i + 1], None, ALU.mult))
            for dst, shift in ((angle, 0.0), (turns, 0.25)):
                step(ve.tensor_scalar(nsin, cos, 1.0 / 6.283185307179586, shift, ALU.mult, ALU.add))
                step(ve.tensor_scalar(nsin, nsin, ROUND, None, ALU.add))
                step(ve.tensor_scalar(nsin, nsin, ROUND, None, ALU.subtract))
                step(ve.scalar_tensor_tensor(dst, nsin, -TWO_PI_HI, cos, ALU.mult, ALU.add))
                step(ve.scalar_tensor_tensor(dst, nsin, -TWO_PI_MID, dst, ALU.mult, ALU.add))
                step(ve.scalar_tensor_tensor(dst, nsin, -TWO_PI_LO, dst, ALU.mult, ALU.add))
                if shift:
                    step(ve.tensor_scalar(dst, dst, 1.5707963267948966, None, ALU.add))
                last = ve.tensor_scalar(dst, dst, 3.1415925, -3.1415925, ALU.min, ALU.max)
                step(last, angles_ready if shift else None)
            dve.wait_ge(sin_ready, 2)
            dve.wait_ge(rstd_ready, 1)
            for i in range(TILES):
                for z in (cos, sin):
                    step(ve.tensor_scalar(z[:, i, :], z[:, i, :], rstd[:, i:i + 1], None, ALU.mult))
            step(ve.tensor_scalar(nsin, sin, -1.0, None, ALU.mult))

            def heads4(ap):
                return ap.rearrange("p (h x f) -> p h x f", h=4, x=2)

            def per_head(ap, n):
                return ap.unsqueeze(1).to_broadcast([P, n, 64])

            for j in range(4):
                n, dst = j % 2, (q if j < 2 else k)
                split_lo(ahead(j))
                dve.wait_ge(piece_used, PARTS * (j + 1))
                for i in range(TILES):
                    src = heads4(ps[:, 2 * n + i, :])
                    step(ve.tensor_tensor(rot_a.rearrange("p (h f) -> p h f", f=64),
                                          ps[:, 2 * n + i, :].rearrange("p (h f) -> p h f", f=64),
                                          per_head(cos[:, i, :], 8), ALU.mult))
                    step(ve.tensor_tensor(heads4(rot_b)[:, :, 0, :], src[:, :, 1, :], per_head(nsin[:, i, :], 4), ALU.mult))
                    step(ve.tensor_tensor(heads4(rot_b)[:, :, 1, :], src[:, :, 0, :], per_head(sin[:, i, :], 4), ALU.mult), read_dve)
                    step(ve.tensor_tensor(dst[:, i, n * N:(n + 1) * N], rot_a, rot_b, ALU.add), rotated)
            dve.wait_ge(const_loaded, 16)
            split_lo(ahead(4))
            split_lo(ahead(5))
            dve.wait_ge(qkT_psum, 8)
            k0 = k[:, 0, :].rearrange("p (h f) -> p h f", f=P)
            step(ve.tensor_tensor(k0, k0, across(const[:, ZETA:ZETA + HEADS], P), ALU.mult), kz_ready)

            def decay_scores(g):
                for c in range(TILES):
                    dve.wait_ge(ret_psum, 5 * g + c + 1)
                    step(ve.tensor_tensor(scoresT[:, c, 0:N], ps[:, 4 + c, :],
                                          const[:, DMAT + g * N:DMAT + (g + 1) * N], ALU.mult), scores_ready)

            def read_ret(g):
                dve.wait_ge(ret_psum, 5 * g + 4)
                step(ve.tensor_copy(ret[:, 0, g * N:(g + 1) * N], ps[:, 4, :]))
                dve.wait_ge(ret_psum, 5 * g + 5)
                step(ve.tensor_tensor(cross.rearrange("p (h f) -> p h f", f=P), bank_cols(7, 4),
                                      across(const[:, XI + 4 * g:XI + 4 * g + 4], P), ALU.mult))
                step(ve.tensor_tensor(ret[:, 1, g * N:(g + 1) * N], cross, ps[:, 5, :], ALU.add), ret_read)

            def silu(j):
                n = j % 2
                for i in range(TILES):
                    dve.wait_ge(sig_g, 2 * (j - 8) + i + 1)
                    z = silu_g[:, i, n * N:(n + 1) * N]
                    step(ve.scalar_tensor_tensor(z, ps[:, 2 * n + i, :], rstd[:, i:i + 1], z, ALU.mult, ALU.mult), read_dve)

            split_lo(ahead(6))
            decay_scores(0)
            split_lo(ahead(7))
            read_ret(0)
            split_lo(ahead(8))
            silu(8)
            decay_scores(1)
            split_lo(ahead(9))
            silu(9)
            read_ret(1)
            flat = [z.rearrange("p t (h f) -> p (t h) f", f=P) for z in (ret, square)]
            step(ve.tensor_reduce(mean, flat[0], AX.X, ALU.add))
            step(ve.tensor_scalar(mean, mean, 1.0 / P, None, ALU.mult))
            step(ve.tensor_tensor(flat[0], flat[0], across(mean, P), ALU.subtract), square_in)
            split_lo(ahead(10))
            dve.wait_ge(squared, 1)
            step(ve.tensor_reduce(var, flat[1], AX.X, ALU.add), var_ready)
            split_lo(ahead(11))
            low(ypoolT_parts, G_POOL, ypT_hi, 0, ypT_ready)
            dve.wait_ge(rstd_ready, 2)
            step(ve.tensor_tensor(flat[0], flat[0], across(var, P), ALU.mult))
            step(ve.tensor_tensor(ret, ret, silu_g, ALU.mult), yret_ready)
            split_lo(ahead(12))
            split_lo(ahead(13))
            low(yretT_parts, G_RET, yrT_hi, 0, yrT_ready)
            dve.wait_ge(read_act, 2 * 8)
            for unit in range(4):
                n, is_a = unit // 2, unit % 2
                split_lo(ahead(BRANCH + unit))
                dve.wait_ge(piece_used, PARTS * (BRANCH + unit + 1))
                for i in range(TILES):
                    m = merged[:, i, n * N:(n + 1) * N]
                    g = gates[1 - is_a][:, i, n * N:(n + 1) * N]
                    final = branch_read if i == TILES - 1 else None
                    if is_a:
                        step(ve.tensor_tensor(branch_tmp, g, ps[:, 2 + i, :], ALU.mult))
                        step(ve.tensor_tensor(m, m, branch_tmp, ALU.add), final)
                    else:
                        step(ve.tensor_tensor(m, g, ps[:, i, :], ALU.mult), final)
                if unit == 3:
                    split_lo(ahead(OUT))
                if unit >= 2:
                    for j in (2 * unit - 4, 2 * unit - 3):
                        dve.wait_ge(mT_hi, j + 1)
                        post(ve.tensor_tensor(mergedT_parts[1][:, 2 * j:2 * j + 2, :], bank_cols(4 + j, 2),
                                              mergedT_parts[0][:, 2 * j:2 * j + 2, :].bitcast(F32), ALU.subtract), mT_ready)
            for n in range(2):
                dve.wait_ge(piece_used, PARTS * OUT + 6 + 2 * n)
                for i in range(TILES):
                    z = x[:, i, n * N:(n + 1) * N]
                    step(ve.tensor_tensor(z, z, ps[:, 2 * n + i, :], ALU.add), x_ready)
            for j in range(2, 4):
                dve.wait_ge(xT_psum, 4 + j + 1)
                post(ve.tensor_tensor(hT[:, 2 * j:2 * j + 2, :], bank_cols(4 + j, 2),
                                      across(vecs[:, G_FFN + 2 * j:G_FFN + 2 * j + 2], SEQ), ALU.mult), hT_ready)
            step(ve.memset(logit[:, :, N_EXPERTS:], BIG))
            step(ve.memset(comb[:, :, N_EXPERTS:], 0.0))
            step(ve.memset(rank[:, :, N_EXPERTS:], 0.0))
            dve.wait_ge(logitT_psum, 1)
            step(ve.tensor_copy(logitT, ps[0:N_EXPERTS, 0, 0:SEQ]), logitT_ready)
            dve.wait_ge(rstd_ready, 3)
            dve.wait_ge(logits_psum, 1)
            for i in range(TILES):
                step(ve.scalar_tensor_tensor(logit[:, i, 0:N_EXPERTS], ps[:, 6, i * N_EXPERTS:(i + 1) * N_EXPERTS],
                                             rstd[:, i:i + 1], b_router, ALU.mult, ALU.add))
            for i in range(TILES):
                step(ve.max(top[:, i, :], logit[:, i, 0:N_EXPERTS]))
            step(ve.tensor_scalar(neg.unsqueeze(2), top[:, :, 0:1], -1.0, None, ALU.mult), exp_in)
            step(ve.memset(top[:, :, TOP_K:8], BIG))
            for i in range(TILES):
                step(ve.match_replace(marked[:, i, :], top[:, i, :], logit[:, i, :], -BIG))
            step(ve.tensor_scalar(mask, marked[:, :, 0:N_EXPERTS], -BIG, None, ALU.is_equal), mask_ready)
            dve.wait_ge(route_psum, 1)
            step(ve.scalar_tensor_tensor(rank[:, :, 0:N_EXPERTS],
                                         ps[:, 4, 0:TILES * N_EXPERTS].rearrange("p (t e) -> p t e", t=TILES), 1.0,
                                         mask, ALU.add, ALU.mult))

            def softmax():
                dve.wait_ge(exp_ready, TILES)
                step(ve.tensor_tensor(expo, expo, mask, ALU.mult))
                step(ve.tensor_reduce(tot, expo, AX.X, ALU.add))
                step(ve.reciprocal(tot, tot))
                step(ve.tensor_tensor(comb[:, :, 0:N_EXPERTS], expo, across(tot, N_EXPERTS), ALU.mult), comb_ready)

            def read_route():
                dve.wait_ge(route_psum, 2)
                step(ve.tensor_copy(combT, ps[0:N_EXPERTS, 7, 0:SEQ]))
                step(ve.tensor_copy(count_f, ps[0:1, 7, SEQ:SEQ + N_EXPERTS]))
                step(ve.tensor_copy(counts, count_f))
                step(ve.tensor_reduce(count_top_f, count_f, AX.X, ALU.max))
                step(ve.tensor_copy(count_top, count_top_f), route_ready)

            def make_onehot(s, experts, lows=(0, 0)):
                for h, (e, low) in enumerate(zip(experts, lows)):
                    for i in range(TILES):
                        last = h == 1 and i == TILES - 1
                        (step if last else post)(ve.tensor_scalar(onehot[:, i, h * BLOCK:(h + 1) * BLOCK],
                                                                  const[:, IOTA + low:IOTA + low + BLOCK],
                                                                  rank[:, i, bass.ds(e, 1)], None, ALU.is_equal),
                                                 s.onehot_ready if last else order[0])

            def make_weighted(s, experts, lows=(0, 0)):
                for h, (e, low) in enumerate(zip(experts, lows)):
                    for i in range(TILES):
                        last = h == 1 and i == TILES - 1
                        step(ve.tensor_scalar(weighted[:, i, h * BLOCK:(h + 1) * BLOCK],
                                              const[:, IOTA + low:IOTA + low + BLOCK],
                                              rank[:, i, bass.ds(e, 1)], comb[:, i, bass.ds(e, 1)],
                                              ALU.is_equal, ALU.mult), s.sw_ready if last else None)

            def read_gather(s, pair):
                dve.wait_ge(s.gathered, pair + 1)
                for b in range(2):
                    g = vecs[:, G_FFN + 4 * b:G_FFN + 4 * b + 4]
                    step(ve.tensor_tensor(hg[:, 4 * b:4 * b + 4, :], bank_cols(6 + b, 4), across(g, P), ALU.mult), s.hg_ready)

            def clamp(s, pair):
                dve.wait_ge(s.chunk_used, PER_PAIR * pair + 2 * UP_CHUNKS)
                step(ve.tensor_scalar(gate, two_banks(0), LIMIT, None, ALU.min), s.gate_ready)
                step(ve.tensor_scalar(up, two_banks(2), LIMIT, -LIMIT, ALU.min, ALU.max), s.up_read)

            def activate(s, pair):
                step(ve.scalar_tensor_tensor(up, up, 1.0, gate, ALU.add, ALU.mult))
                dve.wait_ge(s.sig_ready, pair + 1)
                for half in range(2):
                    columns = slice(half * N, (half + 1) * N)
                    step(ve.tensor_tensor(gate[:, columns], up[:, columns], sig[:, columns], ALU.mult), s.act_ready)

            def read_weights(s, pair):
                dve.wait_ge(s.swt_done, pair + 1)
                step(ve.tensor_copy(scatterT, ps[:, 2, 0:SEQ]), s.st_ready)

            def accumulate(s, pair):
                for i in range(4):
                    dve.wait_ge(s.scattered, 4 * pair + i + 1)
                    n, tile = i // 2, i % 2
                    z = x[:, tile, n * N:(n + 1) * N]
                    step(ve.tensor_tensor(z, z, ps[:, SUM_BANKS[i], :], ALU.add), s.acc_done)

            def pair_steps(pair, is_first=False, is_last=False, has_rest=False):
                if not is_last:
                    make_onehot(first, (2 * pair + 2, 2 * pair + 3))
                make_weighted(first, (2 * pair, 2 * pair + 1))
                clamp(first, pair)
                activate(first, pair)
                if not is_first:
                    accumulate(first, pair - 1)
                read_weights(first, pair)
                if not is_last:
                    read_gather(first, pair + 1)
                if has_rest:
                    read_route()
                    for i in range(4):
                        dve.wait_ge(ple_psum, i + 1)
                        n, tile = i // 2, i % 2
                        step(ve.tensor_copy(ple[:, tile, n * N:(n + 1) * N], ps[:, SUM_BANKS[i], :]), ple_read)
                    for i in range(4):
                        dve.wait_ge(bias_psum, i + 1)
                        n, tile = i // 2, i % 2
                        z = x[:, tile, n * N:(n + 1) * N]
                        step(ve.tensor_tensor(z, z, ps[:, SUM_BANKS[i], :], ALU.add), bias_read)

            make_onehot(first, (0, 1))
            softmax()
            read_gather(first, 0)
            pair_steps(0, is_first=True)

            def per_turn(s, order_sem):
                return {s.onehot_ready: 1, s.sw_ready: 1, s.gate_ready: 1, s.up_read: 1, s.acc_done: 4,
                        s.act_ready: 2, s.hg_ready: 2, s.st_ready: 1, order_sem: 3 + 3 + 1}

            turn = per_turn(first, vec_order)

            def inner_pairs(begin, end):
                with dve.Fori(begin, end) as pair:
                    for s, n in turn.items():
                        own(s).enter(pair - begin, n)
                    pair_steps(pair)
                    for s in turn:
                        own(s).leave(end - begin)

            inner_pairs(1, REST_PAIR)
            pair_steps(REST_PAIR, has_rest=True)
            inner_pairs(REST_PAIR + 1, PAIRS - 1)
            pair_steps(PAIRS - 1, is_last=True)
            accumulate(first, PAIRS - 1)

            more_turn = per_turn(more, more.order)

            def body(j, e, low):
                for s, n in more_turn.items():
                    own(s).n, own(s).base = 0, j * n
                make_onehot(more, (e, e), (low, low + BLOCK))
                make_weighted(more, (e, e), (low, low + BLOCK))
                read_gather(more, j)
                clamp(more, j)
                activate(more, j)
                read_weights(more, j)
                accumulate(more, j)
                dve.sem_inc(more.pair_done, 1)
                for s, n in more_turn.items():
                    assert own(s).n == n, (s, own(s).n, n)

            def skipped():
                for s, n in more_turn.items():
                    dve.sem_inc(s, n)
                dve.sem_inc(more.pair_done, 1)

            order[0] = more.order
            more_pairs("dve", dve, body, skipped)
            order[0] = vec_order

            dve.sem_inc(x_ready, 4)
            own(x_ready).n += 4
            split_lo(PARTS * PLE_BLOCK + 1)
            for part in range(PARTS):
                low(hT_parts, G_PLE, hT_hi, KD, hT_ready, 0, (2 * part, 2 * part + 1))
                split_lo(PARTS * PLE_BLOCK + part + 2)
            split_lo(PARTS * PLE_BLOCK + 2 * PARTS)

            def add_embedding(n, i):
                dve.wait_ge(gate_sig, 2 * n + i + 1)
                z = x[:, i, n * N:(n + 1) * N]
                g = ple_gate[:, n, i, :]
                step(ve.tensor_tensor(g, g, ple[:, i, n * N:(n + 1) * N], ALU.mult))
                step(ve.tensor_tensor(z, z, g, ALU.add), x_ready)

            for i in range(TILES):
                add_embedding(0, i)
            for i in range(TILES):
                post(ve.tensor_tensor(result[:, i, 0:N], x[:, i, 0:N], g_final[:, 0:N], ALU.mult), scaled_gain)
            for i in range(TILES):
                add_embedding(1, i)
                dve.wait_ge(rstd_ready, 5 + i)
                post(ve.scalar_tensor_tensor(result[:, i, N:2 * N], x[:, i, N:2 * N], rstd[:, i:i + 1], g_final[:, N:2 * N],
                                             ALU.mult, ALU.mult), out_ready)


def constants():
    import numpy as np
    c = np.zeros((P, N_CONST), np.float32)
    r = np.arange(P)
    c[:, IDENT:IDENT + P] = np.eye(P)
    c[:, INVF:INVF + 64] = np.power(np.float32(10000.0), -(np.arange(64, dtype=np.float32) / np.float32(64)))
    c[:, TRI:TRI + P] = r[:, None] < r[None, :]
    c[:, ONES:ONES + P] = 1.0
    c[:, IOTA:DMAT] = np.arange(1, DMAT - IOTA + 1)
    scale = float(P) ** -0.5
    log_gamma = np.log1p(-np.exp2(-5.0 - np.arange(HEADS)))
    for h in range(HEADS):
        d = r[None, :] - r[:, None]
        c[:, DMAT + h * P:DMAT + (h + 1) * P] = np.where(d >= 0, np.exp(log_gamma[h] * np.maximum(d, 0)) * scale, 0)
        c[:, ZETA + h] = np.exp(log_gamma[h] * (P - 1 - r)) * scale
        c[:, XI + h] = np.exp(log_gamma[h] * (r + 1))
    for h in range(2):
        c[h, SEL + h * BLOCK:SEL + (h + 1) * BLOCK] = 1.0
    pos = np.arange(SEQ)
    for i, w in enumerate(WINDOWS):
        lag = pos[None, :] - pos[:, None]
        m = ((lag >= 0) & (lag < w)) / np.minimum(pos + 1, w)[None, :] - np.eye(SEQ)
        at = POOLM + 3 * P * i
        c[:, at:at + P], c[:, at + P:at + 2 * P], c[:, at + 2 * P:at + 3 * P] = m[:P, :P], m[:P, P:], m[P:, P:]
    return c


_INS = ["x", "p", "positions", "g_mix_norm", "w_in", "g_ret_norm", "w_pool", "pool_scale", "w_branch", "w_out",
        "g_ffn_norm", "w_router", "b_router", "w_gate_up", "b_gate_up", "w_down", "b_down", "g_ple_norm",
        "w_ple_gate", "w_ple_proj", "g_final"]


def kernel(**inputs):
    import numpy as np
    import concourse.bacc as bacc
    from concourse.bass_utils import run_bass_kernel_spmd

    nc = bacc.Bacc("TRN2", target_bir_lowering=False, num_devices=1)
    arrays = {f"in_{n}": np.ascontiguousarray(inputs[n]) for n in _INS}
    arrays["in_const"] = constants()
    tensors = {n[3:]: nc.dram_tensor(n, a.shape, mybir.dt.from_np(a.dtype), kind="ExternalInput").ap()
               for n, a in arrays.items()}
    tensors["y"] = nc.dram_tensor("out_y", (1, SEQ, D), F32, kind="ExternalOutput").ap()
    build(nc, tensors)
    return run_bass_kernel_spmd(nc, [arrays], core_ids=[0]).results[0]["out_y"]
```
